# Optimizing a Trainium2 kernel written in Bass

```python
import jax, jax.numpy as jnp
from jax import lax
import numpy as np

D_MODEL = 1024
BATCH = 1
SEQ = 512
DEPTH = 1
DEC_BATCH = 1
DEC_SEQ = 1024
PAST_LEN = 128

GRID_W = 64
HEAD_DIM = 64
N_Q_HEADS = 8
N_KV_HEADS = 2
Q_PER_KV = N_Q_HEADS // N_KV_HEADS
ATTN_WIDTH = N_Q_HEADS * HEAD_DIM
KV_WIDTH = N_KV_HEADS * HEAD_DIM
POOL_WINDOWS = (2, 4, 8, 16)
N_POOL_GROUPS = len(POOL_WINDOWS)
POOL_WIDTH = D_MODEL - ATTN_WIDTH
POOL_GROUP_DIM = POOL_WIDTH // N_POOL_GROUPS
MIX_WIDTH = ATTN_WIDTH + POOL_WIDTH
IN_WIDTH = ATTN_WIDTH + 2 * KV_WIDTH + POOL_WIDTH
D_FF = 4 * D_MODEL
Q_BLOCK = 128
ROPE_THETA = 10000.0
EPS = 1e-6

kernel_name = "hymba_attn_pool_encoder"

def rmsnorm(x, g):
    xf = x.astype(jnp.float32)
    y = xf * lax.rsqrt(jnp.mean(xf * xf, axis=-1, keepdims=True) + EPS) * g.astype(jnp.float32)
    return y.astype(x.dtype)

def axial_rope_tables(seq_len):
    rows = seq_len // GRID_W
    row_ids = jnp.broadcast_to(jnp.arange(rows, dtype=jnp.float32)[:, None], (rows, GRID_W)).reshape(-1)
    col_ids = jnp.broadcast_to(jnp.arange(GRID_W, dtype=jnp.float32)[None, :], (rows, GRID_W)).reshape(-1)
    n_freq = HEAD_DIM // 4
    inv_freq = ROPE_THETA ** (-jnp.arange(n_freq, dtype=jnp.float32) / n_freq)
    ang = jnp.stack([row_ids[:, None] * inv_freq, col_ids[:, None] * inv_freq], axis=1)
    return jnp.cos(ang), jnp.sin(ang)

def apply_axial_rope(x, cos, sin):
    B, S, H, _ = x.shape
    xr = x.reshape(B, S, H, 2, 2, HEAD_DIM // 4)
    x1, x2 = xr[..., 0, :], xr[..., 1, :]
    c = cos[None, :, None].astype(x.dtype)
    s = sin[None, :, None].astype(x.dtype)
    out = jnp.stack([x1 * c - x2 * s, x2 * c + x1 * s], axis=-2)
    return out.reshape(B, S, H, HEAD_DIM)

def block_swept_gqa(q, k, v):
    B, S = q.shape[:2]
    nblk = S // Q_BLOCK
    scale = HEAD_DIM ** -0.5
    qb = q.reshape(B, nblk, Q_BLOCK, N_KV_HEADS, Q_PER_KV, HEAD_DIM).transpose(1, 0, 2, 3, 4, 5)

    def one_block(qi):
        s = jnp.einsum('bqkgd,bskd->bkgqs', qi, k, preferred_element_type=jnp.float32) * scale
        p = jax.nn.softmax(s, axis=-1).astype(v.dtype)
        return jnp.einsum('bkgqs,bskd->bqkgd', p, v)

    ob = lax.map(one_block, qb)
    return ob.transpose(1, 0, 2, 3, 4, 5).reshape(B, S, ATTN_WIDTH)

def multiscale_pool(u, w_pool, pool_scale):
    B, S, _ = u.shape
    uf = u.astype(jnp.float32).reshape(B, S, N_POOL_GROUPS, POOL_GROUP_DIM)
    cs = jnp.concatenate([jnp.zeros((B, 1, N_POOL_GROUPS, POOL_GROUP_DIM), jnp.float32),
                          jnp.cumsum(uf, axis=1)], axis=1)
    t = jnp.arange(S)[:, None]
    win = jnp.array(POOL_WINDOWS, dtype=jnp.int32)[None, :]
    lo = jnp.clip(t - win // 2, 0, S)
    hi = jnp.clip(t - win // 2 + win, 0, S)
    cnt = (hi - lo).astype(jnp.float32)
    g_idx = jnp.arange(N_POOL_GROUPS)[None, :]
    wsum = cs[:, hi, g_idx, :] - cs[:, lo, g_idx, :]
    d = wsum / cnt[None, :, :, None] - uf
    z = jnp.einsum('bsgc,gce->bsge', d, w_pool.astype(jnp.float32))
    z = z.reshape(B, S, POOL_WIDTH) * pool_scale.astype(jnp.float32)
    return z.astype(u.dtype)

def encoder_layer(x, norm1_g, w_in, q_norm_g, k_norm_g, w_pool, pool_scale, w_out,
                  norm2_g, w_up, w_down, cos, sin):
    B, S, _ = x.shape
    h = rmsnorm(x, norm1_g)
    proj = h @ w_in
    q = proj[..., :ATTN_WIDTH].reshape(B, S, N_Q_HEADS, HEAD_DIM)
    k = proj[..., ATTN_WIDTH:ATTN_WIDTH + KV_WIDTH].reshape(B, S, N_KV_HEADS, HEAD_DIM)
    v = proj[..., ATTN_WIDTH + KV_WIDTH:ATTN_WIDTH + 2 * KV_WIDTH].reshape(B, S, N_KV_HEADS, HEAD_DIM)
    u = proj[..., ATTN_WIDTH + 2 * KV_WIDTH:]
    q = apply_axial_rope(rmsnorm(q, q_norm_g), cos, sin)
    k = apply_axial_rope(rmsnorm(k, k_norm_g), cos, sin)
    a = block_swept_gqa(q, k, v)
    p = multiscale_pool(u, w_pool, pool_scale)
    x = x + jnp.concatenate([a, p], axis=-1) @ w_out
    h2 = rmsnorm(x, norm2_g)
    x = x + jnp.square(jax.nn.relu(h2 @ w_up)) @ w_down
    return x

def run_trunk(x, norm1_g, w_in, q_norm_g, k_norm_g, w_pool, pool_scale, w_out,
              norm2_g, w_up, w_down):
    cos, sin = axial_rope_tables(x.shape[1])
    for l in range(DEPTH):
        x = encoder_layer(x, norm1_g[l], w_in[l], q_norm_g[l], k_norm_g[l], w_pool[l],
                          pool_scale[l], w_out[l], norm2_g[l], w_up[l], w_down[l], cos, sin)
    return x

def setup_inputs(seed: int = 0) -> dict:
    key = jax.random.key(seed)
    ks = jax.random.split(key, 13)
    f32 = jnp.float32

    def nrm(k, shape, scale):
        return jax.random.normal(k, shape, f32) * scale

    return {
        "x_prompt": nrm(ks[0], (BATCH, SEQ, D_MODEL), 1.0),
        "x_sample": nrm(ks[1], (DEC_BATCH, DEC_SEQ, D_MODEL), 1.0),
        "norm1_g": 1.0 + nrm(ks[2], (DEPTH, D_MODEL), 0.05),
        "w_in": nrm(ks[3], (DEPTH, D_MODEL, IN_WIDTH), D_MODEL ** -0.5),
        "q_norm_g": 1.0 + nrm(ks[4], (DEPTH, HEAD_DIM), 0.05),
        "k_norm_g": 1.0 + nrm(ks[5], (DEPTH, HEAD_DIM), 0.05),
        "w_pool": nrm(ks[6], (DEPTH, N_POOL_GROUPS, POOL_GROUP_DIM, POOL_GROUP_DIM), POOL_GROUP_DIM ** -0.5),
        "pool_scale": 1.0 + nrm(ks[7], (DEPTH, POOL_WIDTH), 0.1),
        "w_out": nrm(ks[8], (DEPTH, MIX_WIDTH, D_MODEL), MIX_WIDTH ** -0.5),
        "norm2_g": 1.0 + nrm(ks[9], (DEPTH, D_MODEL), 0.05),
        "w_up": nrm(ks[10], (DEPTH, D_MODEL, D_FF), D_MODEL ** -0.5),
        "w_down": nrm(ks[11], (DEPTH, D_FF, D_MODEL), D_FF ** -0.5),
    }

def reference(x_prompt, x_sample, norm1_g, w_in, q_norm_g, k_norm_g, w_pool, pool_scale,
              w_out, norm2_g, w_up, w_down):
    y_prompt = run_trunk(x_prompt, norm1_g, w_in, q_norm_g, k_norm_g, w_pool, pool_scale,
                         w_out, norm2_g, w_up, w_down)
    y_sample = run_trunk(x_sample, norm1_g, w_in, q_norm_g, k_norm_g, w_pool, pool_scale,
                         w_out, norm2_g, w_up, w_down)
    return (y_prompt, y_sample)


_drawn_inputs = setup_inputs


def setup_inputs(seed=0):
    import zlib

    import numpy as np

    out = dict(_drawn_inputs(seed))
    spreads = {}
    factors = {'q_norm_g': 8.0, 'k_norm_g': 8.0}
    for name, (base, spread) in spreads.items():
        noise = np.random.default_rng([zlib.crc32(name.encode()), seed]).standard_normal(out[name].shape)
        drawn = base * np.exp(spread * noise) if base else spread * noise
        out[name] = __import__('jax').numpy.asarray(drawn.astype(out[name].dtype))
    for name, factor in factors.items():
        out[name] = (out[name] * factor).astype(out[name].dtype)
    return out
```

```python
from contextlib import ExitStack

import numpy as np

import concourse.bass as bass
from concourse import mybir

ALU = mybir.AluOpType
ACT = mybir.ActivationFunctionType
AX = mybir.AxisListType
F32 = mybir.dt.float32
F32R = mybir.dt.float32r

P = 128
D = 1024
KT = D // P
HEAD = 64
NQ, NKV = 8, 2
NQK = NQ + NKV
ATT = NQ * HEAD
QKW = NQK * HEAD
QKVW = ATT + 2 * NKV * HEAD
GROUPS = 4
WINDOWS = (2, 4, 8, 16)
INW = QKVW + GROUPS * P
SEQ_P, SEQ_S = 512, 1024
T = SEQ_P + SEQ_S
TT = T // P
NB = T // 512
FF = 4 * D
FC = 256
FT = FC // P
NCH = FF // FC
PAD = 8
EPS = 1e-6
SCALE = HEAD ** -0.5
THETA = 10000.0
GRID_W = 64
SEQS = ((0, SEQ_P), (SEQ_P, SEQ_S))
UP0 = (0, SEQ_P + 2 * PAD)
UPW = T + 4 * PAD


def hybrid_layer(nc, x, g1, w_in, gqk, w_pool, pool_scale, w_out, g2, w_up, w_down,
                 ident_d, rope_d, edge_d, y):
    with ExitStack() as ctx:
        def sem(name):
            return ctx.enter_context(nc.semaphore(name))

        def at(name, off, shape, dt=F32):
            return nc.alloc_sbuf_tensor_at(name, [P] + shape, dt, offset=BASE + off)

        BASE = 640
        ident = at("ident", 0, [P])
        edge = at("edge", 512, [GROUPS, 2 * PAD])
        pscale = at("pscale", 768, [GROUPS])
        ssx = at("ssx", 800, [1])
        rsx = at("rsx", 832, [1])
        ssqk = at("ssqk", 864, [NQK])
        rsqk = at("rsqk", 928, [NQK])
        mexp = at("mexp", 992, [NQK])
        nmax = at("nmax", 1056, [2, 4])
        rsum = at("rsum", 1088, [2, 4])
        rinv = at("rinv", 1120, [2, 4])
        msx = at("msx", 1152, [1])
        msqk = at("msqk", 1184, [NQK])
        epsx = at("epsx", 1248, [1])
        epsqk = at("epsqk", 1280, [NQK])
        rcopy = at("rcopy", 1344, [2, 4])
        M = 1536
        X = M
        concat = at("concat", X, [KT, T])
        h2hi = at("h2hi", X, [KT, T], F32R)
        g1b = at("g1b", X, [D])
        gqkb = at("gqkb", X + 4096, [NQK, HEAD])
        rope = at("rope", X + 6656, [2, 2, HEAD])
        wraw = at("wraw", X + 8704, [2, INW])
        qn = at("qn", X + 8704, [NQK, HEAD])
        qsin = at("qsin", X + 11264, [NQK, HEAD])
        roped = at("roped", X + 13824, [2, NQK, HEAD])
        junk = at("junk", X + 18944, [D])
        up = at("up", X + 24576, [GROUPS, UPW])
        R = X + 24576 + 4 * GROUPS * UPW
        QT = at("QT", R, [5, T])
        V = at("V", R + 30720, [TT, NKV, 2 * HEAD], F32R)
        S = R + 43008
        wihi = at("wihi", S, [KT, INW], F32R)
        wilo = at("wilo", S + 40960, [KT, INW], F32R)
        hThi = at("hThi", S + 81920, [2, KT, 256], F32R)
        hTlo = at("hTlo", S + 81920 + 16384, [2, KT, 256], F32R)
        W = S + 114688
        xin = at("xin", W, [2, D])
        xs = at("xs", W + 8192, [D])
        qk = at("qk", W + 12288, [NQK, HEAD])
        qksq = at("qksq", W + 14848, [NQK, HEAD])
        KA = at("KA", S, [NKV, T], F32R)
        KB = at("KB", S + 12288, [NKV, T], F32R)
        prob = at("prob", S + 24576, [2, 4, SEQ_S])
        pThi = at("pThi", S + 57344, [2, 512], F32R)
        pTlo = at("pTlo", S + 61440, [2, 512], F32R)
        Qs = at("Qs", S + 65536, [2, 512], F32R)
        Vg = at("Vg", S + 69632, [SEQ_S // P, 2 * HEAD], F32R)
        half_o = at("half_o", S + 73728, [512])
        sw = at("sw", S + 75776, [2, SEQ_S + 2 * PAD])
        wp_raw = at("wp_raw", S + 84224, [GROUPS, P])
        wphi = at("wphi", S + 86272, [GROUPS, P], F32R)
        wplo = at("wplo", S + 88320, [GROUPS, P], F32R)
        dhi = at("dhi", S + 90368, [2, 512], F32R)
        dlo = at("dlo", S + 94464, [2, 512], F32R)
        woraw = at("woraw", S + 98560, [KT, D])
        h2lo = at("h2lo", R, [KT, T], F32R)
        R2 = R + 49152
        wohi = at("wohi", R2, [KT, D], F32R)
        wolo = at("wolo", R2 + 32768, [KT, D], F32R)
        C = R2 + 65536
        chi = at("chi", C, [2, KT, P], F32R)
        clo = at("clo", C + 8192, [2, KT, P], F32R)
        xs2 = at("xs2", C + 16384, [D])
        g2b = at("g2b", C + 20480, [D])
        x2in = at("x2in", C + 49152, [2, D])
        yacc = at("yacc", R2, [TT, D])
        wdhi = at("wdhi", R2 + 49152, [FT, D], F32R)
        wdlo = at("wdlo", R2 + 57344, [FT, D], F32R)
        hid_hi = at("hid_hi", C, [3, FT, 512], F32R)
        hid_lo = at("hid_lo", C + 12288, [3, FT, 512], F32R)
        wuhi = at("wuhi", C + 24576, [KT, FC], F32R)
        wulo = at("wulo", C + 32768, [KT, FC], F32R)
        wuraw = at("wuraw", C + 40960, [KT, FC])
        wdraw = at("wdraw", C + 49152, [FT, D])
        relu = at("relu", C + 57344, [512])
        hsq = at("hsq", C + 59392, [512])

        ps = ctx.enter_context(nc.psum_tensor("ps", [P, 8, 512], F32))
        psw = ps[:].rearrange("p b c -> p (b c)")

        const_in = sem("const_in")
        w_in_in = [sem("w_in_in0"), sem("w_in_in1")]
        x_in = [sem("x_in0"), sem("x_in1")]
        rope_in = [sem("rope_in0"), sem("rope_in1")]
        wi_hi = sem("wi_hi")
        wi_lo = sem("wi_lo")
        g1_scaled = sem("g1_scaled")
        g2_scaled = sem("g2_scaled")
        inv_seen = sem("inv_seen")
        gq_scaled = sem("gq_scaled")
        pads = sem("pads")
        mexp_set = sem("mexp_set")
        ssx_done = sem("ssx_done")
        msx_done = sem("msx_done")
        rsx_done = sem("rsx_done")
        xs_done = sem("xs_done")
        xT_done = sem("xT_done")
        hT_hi = sem("hT_hi")
        hT_lo = sem("hT_lo")
        qkv_done = sem("qkv_done")
        u_done = sem("u_done")
        u_saved = sem("u_saved")
        qk_copied = sem("qk_copied")
        qk_squared = sem("qk_squared")
        v_hi = sem("v_hi")
        v_lo = sem("v_lo")
        qk_summed = sem("qk_summed")
        msqk_done = sem("msqk_done")
        rsqk_done = sem("rsqk_done")
        qn_done = sem("qn_done")
        qg_done = sem("qg_done")
        cos_done = sem("cos_done")
        sin_done = sem("sin_done")
        rope_done = sem("rope_done")
        qkT_done = sem("qkT_done")
        qkT_saved = sem("qkT_saved")

        win_step = sem("win_step")
        win_done = sem("win_done")
        d_done = sem("d_done")
        k_hi = sem("k_hi")
        k_lo = sem("k_lo")
        k_dup = sem("k_dup")
        vg_done = sem("vg_done")
        q_hi = sem("q_hi")
        q_lo = sem("q_lo")
        s_done = sem("s_done")
        max_done = sem("max_done")
        exp_done = sem("exp_done")
        inv_done = sem("inv_done")
        norm_done = sem("norm_done")
        pT_done = sem("pT_done")
        pT_hi = sem("pT_hi")
        pT_lo = sem("pT_lo")
        pv_done = sem("pv_done")
        o_half = sem("o_half")
        o_saved = sem("o_saved")

        wp_in = sem("wp_in")
        wp_hi = sem("wp_hi")
        wp_lo = sem("wp_lo")
        d_hi = sem("d_hi")
        d_lo = sem("d_lo")
        z_done = sem("z_done")
        z_saved = sem("z_saved")
        wo_in = sem("wo_in")
        wo_hi = sem("wo_hi")
        wo_lo = sem("wo_lo")
        g2_in = sem("g2_in")
        x2_in = [sem(f"x2_in{i}") for i in range(2)]
        c_hi = sem("c_hi")
        c_lo = sem("c_lo")
        out_done = sem("out_done")
        x2_done = sem("x2_done")
        x2_stored = [sem(f"x2_stored{i}") for i in range(2)]
        ss2_done = sem("ss2_done")
        ms2_done = sem("ms2_done")
        rs2_done = sem("rs2_done")
        xs2_done = sem("xs2_done")
        xT2_done = sem("xT2_done")
        h2_hi = sem("h2_hi")
        h2_lo = sem("h2_lo")

        y_in = [sem(f"y_in{b}") for b in range(NB)]
        wu_in = sem("wu_in")
        wd_in = sem("wd_in")
        wu_hi = sem("wu_hi")
        wu_lo = sem("wu_lo")
        wd_hi = sem("wd_hi")
        wd_lo = sem("wd_lo")
        up_done = sem("up_done")
        relu_done = sem("relu_done")
        sq_done = sem("sq_done")
        hid_hi_done = sem("hid_hi_done")
        hid_lo_done = sem("hid_lo_done")
        down_done = sem("down_done")
        acc_done = sem("acc_done")
        y_out = sem("y_out")

        block = ctx.enter_context(nc.Block())

        class Seq:
            def __init__(self, n, jobs_before, tiles_before):
                self.n = n
                self.start, self.len = SEQS[n]
                self.nk = self.len // 512
                self.nkt = self.len // P
                self.jobs = [(qb, half) for qb in range(self.nk) for half in range(2)]
                self.per = len(self.jobs)
                self.j0 = jobs_before
                self.t0 = tiles_before

            def job(self, pair, idx):
                return self.j0 + pair * self.per + idx

            def tile(self, pair, idx, kt):
                return self.t0 + (pair * self.per + idx) * self.nkt + kt

        seqs = [Seq(0, 0, 0), Seq(1, 8, 8 * (SEQ_P // P))]
        JOBS = 8 + 16

        def qk_slots(s):
            return {0: [0, 1], 1: [2, 3]} if s.nk == 1 else {0: [0], 1: [1], 2: [2], 3: [3]}

        def pair_kv(pair):
            return pair // (NQ // 2 // NKV)

        def later_job(s, pair, idx, ahead):
            pair, idx = pair + (idx + ahead) // s.per, (idx + ahead) % s.per
            if isinstance(pair, int) and pair >= NQ // 2:
                if s.n == 1:
                    return None
                over = (pair - NQ // 2) * s.per + idx
                return seqs[1], over // seqs[1].per, over % seqs[1].per
            return s, pair, idx

        def pool_pos(s):
            return UP0[s] + PAD

        @block.sync
        def _(sp):
            sp.dma_start(xin[:, 0], x[0:P]).then_inc(x_in[0], 16)
            sp.dma_start(g1b[:], g1.partition_broadcast(P)).then_inc(const_in, 16)
            sp.dma_start(ident[:], ident_d).then_inc(const_in, 16)
            sp.dma_start(xin[:, 1], x[P:2 * P]).then_inc(x_in[1], 16)
            sp.dma_start(gqkb[:], gqk.partition_broadcast(P)).then_inc(const_in, 16)
            sp.dma_start(edge[:], edge_d).then_inc(const_in, 16)
            sp.dma_start(pscale[:], pool_scale).then_inc(const_in, 16)
            for k in range(KT):
                if k >= 2:
                    sp.wait_ge(wi_hi, k - 1)
                    sp.wait_ge(wi_lo, k - 1)
                sp.dma_start(wraw[:, k % 2], w_in[k * P:(k + 1) * P]).then_inc(w_in_in[k % 2], 16)
            sp.dma_start(rope[:, 0], rope_d[0]).then_inc(rope_in[0], 16)
            sp.dma_start(rope[:, 1], rope_d[1]).then_inc(rope_in[1], 16)

            def load_x(t, i):
                sp.wait_ge(xs_done, t - 1)
                sp.dma_start(xin[:, i], x[bass.ds(t * P, P)]).then_inc(x_in[i], 16)

            def load_rope(t, i):
                sp.wait_ge(cos_done, t - 1)
                sp.wait_ge(sin_done, t - 1)
                sp.dma_start(rope[:, i], rope_d[bass.ds(t, 1)].rearrange("a p c h -> (a p) c h")
                             ).then_inc(rope_in[i], 16)

            load_x(2, 0)
            load_x(3, 1)
            with sp.Fori(2, TT // 2) as h:
                for i in range(2):
                    load_x(h * 2 + i, i)
                    load_rope(h * 2 + i - 2, i)
            load_rope(TT - 2, 0)
            load_rope(TT - 1, 1)
            sp.wait_ge(u_done, TT // 2)
            sp.wait_ge(xT_done, TT)
            sp.wait_ge(rope_done, TT)
            sp.dma_start(wp_raw[:], w_pool.rearrange("g c e -> c g e")).then_inc(wp_in, 16)
            sp.dma_start(woraw[:], w_out.rearrange("(k p) n -> p k n", p=P)).then_inc(wo_in, 16)
            sp.wait_ge(z_done, GROUPS * NB)
            sp.dma_start(g2b[:], g2.partition_broadcast(P)).then_inc(g2_in, 16)
            sp.wait_ge(wo_hi, KT)
            sp.wait_ge(wo_lo, KT)
            for i in range(2):
                sp.dma_start(x2in[:, i], x[i * P:(i + 1) * P]).then_inc(x2_in[i], 16)
            sp.dma_start(wuraw[:], w_up[0]).then_inc(wu_in, 16)
            with sp.Fori(0, TT // 2 - 1) as h:
                t = h * 2
                for i in range(2):
                    sp.wait_ge(x2_done, t + i + 1)
                    sp.dma_start(y[bass.ds((t + i) * P, P)], x2in[:, i]).then_inc(x2_stored[i], 16)
                for i in range(2):
                    sp.wait_ge(x2_stored[i], t * 8 + 16)
                    sp.wait_ge(xs2_done, t + i + 1)
                    sp.dma_start(x2in[:, i], x[bass.ds((t + i + 2) * P, P)]).then_inc(x2_in[i], 16)
            for i in range(2):
                sp.wait_ge(x2_done, TT - 1 + i)
                sp.dma_start(y[(TT - 2 + i) * P:(TT - 1 + i) * P], x2in[:, i]).then_inc(x2_stored[i], 16)
            sp.wait_ge(x2_stored[0], 8 * TT)
            sp.wait_ge(x2_stored[1], 8 * TT)
            sp.wait_ge(out_done, TT)
            for b in range(NB):
                sp.dma_start(yacc[:, 4 * b:4 * b + 4],
                             y[b * 512:(b + 1) * 512].rearrange("(t p) n -> p t n", p=P)).then_inc(y_in[b], 16)
            sp.wait_ge(xs2_done, TT)
            sp.dma_start(wdraw[:], w_down[0:FC].rearrange("(f p) n -> p f n", p=P)).then_inc(wd_in, 16)
            with sp.Fori(1, NCH) as c:
                sp.wait_ge(wu_hi, c)
                sp.wait_ge(wu_lo, c)
                sp.dma_start(wuraw[:], w_up[bass.ds(c, 1)].rearrange("a p k f -> (a p) k f")).then_inc(wu_in, 16)
                sp.wait_ge(wd_hi, c)
                sp.wait_ge(wd_lo, c)
                sp.dma_start(wdraw[:], w_down[bass.ds(c * FC, FC)].rearrange("(f p) n -> p f n", p=P)
                             ).then_inc(wd_in, 16)
            for b in range(NB):
                sp.wait_ge(acc_done, (NCH - 1) * TT + 4 * (b + 1))
                sp.dma_start(y[b * 512:(b + 1) * 512].rearrange("(t p) n -> p t n", p=P),
                             yacc[:, 4 * b:4 * b + 4]).then_inc(y_out, 16)
            sp.wait_ge(y_out, 16 * NB)

        @block.tensor
        def _(pe):
            def three(out, w_hi, w_lo, m_hi, m_lo, start, stop):
                pe.matmul(out, w_hi, m_hi, start=start, stop=False)
                pe.matmul(out, w_hi, m_lo, start=False, stop=False)
                return pe.matmul(out, w_lo, m_hi, start=False, stop=stop)

            def transpose_x(t):
                pe.wait_ge(xs_done, t + 1)
                pe.wait_ge(hT_lo, t)
                for k in range(KT):
                    mm = pe.transpose(psw[:, k * P:(k + 1) * P], xs[:, k * P:(k + 1) * P], ident[:])
                mm.then_inc(xT_done, 1)

            def project_qkv(t, i):
                buf, tok = i // 2, (i % 2) * P
                pe.wait_ge(hT_lo, t + 1)
                pe.wait_ge(qk_copied, t)
                pe.wait_ge(v_lo, t)
                for out, c0, c1 in ((ps[:, 2, :], 0, 512), (ps[:, 3, 0:QKVW - 512], 512, QKVW)):
                    for k in range(KT):
                        mm = three(out, hThi[:, buf, k, tok:tok + P], hTlo[:, buf, k, tok:tok + P],
                                   wihi[:, k, c0:c1], wilo[:, k, c0:c1], k == 0, k == KT - 1)
                mm.then_inc(qkv_done, 1)

            def project_u(p, buf):
                pe.wait_ge(u_saved, p)
                for g in range(GROUPS):
                    c0 = QKVW + g * P
                    for k in range(KT):
                        mm = three(ps[:, 4 + g // 2, (g % 2) * 256:(g % 2) * 256 + 256],
                                   wihi[:, k, c0:c0 + P], wilo[:, k, c0:c0 + P],
                                   hThi[:, buf, k, :], hTlo[:, buf, k, :], k == 0, k == KT - 1)
                mm.then_inc(u_done, 1)

            def transpose_qk(t, i):
                pe.wait_ge(rope_done, t + 1)
                pe.wait_ge(qkT_saved, t)
                for j in range(5):
                    mm = pe.transpose(psw[:, 3072 + j * P:3072 + (j + 1) * P],
                                      roped[:, i % 2, 2 * j:2 * j + 2].rearrange("p h d -> p (h d)"), ident[:])
                mm.then_inc(qkT_done, 1)

            def project_block(n, last):
                for i in range(4):
                    t = n * 4 + i
                    project_qkv(t, i)
                    if not (last and i >= 2):
                        transpose_x(t + 2)
                    if i % 2:
                        project_u(n * 2 + i // 2, i // 2)
                        transpose_qk(t - 1, i - 1)
                        transpose_qk(t, i)

            pe.wait_ge(const_in, 5 * 16)
            transpose_x(0)
            transpose_x(1)
            pe.wait_ge(wi_hi, KT)
            pe.wait_ge(wi_lo, KT)
            with pe.Fori(0, NB - 1) as n:
                project_block(n, False)
            project_block(NB - 1, True)

            def scores(s, pair, idx, qt):
                j = s.job(pair, idx)
                if qt == 0:
                    pe.wait_ge(q_lo, j + 1)
                if not isinstance(j, int) or j > 0 or qt >= 2:
                    pe.wait_ge(exp_done, 4 * j + qt - 1)
                for h in range(s.nk):
                    key0 = s.start + h * 512
                    out = ps[:, 2 * (qt % 2) + h]
                    q = Qs[:, idx % 2, qt * P:(qt + 1) * P]
                    kv = pair_kv(pair)
                    pe.matmul(out, q, KA[:, bass.ds(kv, 1), key0:key0 + 512].rearrange("p a c -> p (a c)"),
                              start=True, stop=False)
                    mm = pe.matmul(out, q, KB[:, bass.ds(kv, 1), key0:key0 + 512].rearrange("p a c -> p (a c)"),
                                   start=False, stop=True)
                mm.then_inc(s_done, 1)

            def transpose_p(s, pair, idx, kt):
                if kt == 0:
                    pe.wait_ge(norm_done, 4 * s.job(pair, idx) + 4)
                for qt in range(4):
                    mm = pe.transpose(ps[:, 4 + kt % 2, qt * P:(qt + 1) * P],
                                      prob[:, idx % 2, qt, kt * P:(kt + 1) * P], ident[:])
                mm.then_inc(pT_done, 1)

            def values(s, pair, idx, kt):
                pe.wait_ge(pT_lo, s.tile(pair, idx, kt) + 1)
                if kt == 0:
                    pe.wait_ge(vg_done, NQ // 2 * s.n + pair + 1)
                out = ps[:, 6 + idx % 2]
                pe.matmul(out, Vg[:, kt], pThi[:, kt % 2], start=(kt == 0), stop=False)
                pe.matmul(out, Vg[:, kt], pTlo[:, kt % 2], start=False, stop=(kt == s.nkt - 1)
                          ).then_inc(pv_done, 1)

            def attend_pair(s, pair):
                for idx in range(s.per):
                    nxt = later_job(s, pair, idx, 1)
                    for kt in range(s.nkt):
                        transpose_p(s, pair, idx, kt)
                        if kt:
                            if nxt:
                                for qt in qk_slots(s).get(kt - 1, []):
                                    scores(*nxt, qt)
                            values(s, pair, idx, kt - 1)
                    values(s, pair, idx, s.nkt - 1)

            pe.wait_ge(k_dup, 2)
            for qt in range(4):
                scores(seqs[0], 0, 0, qt)
            for s in seqs:
                with pe.Fori(0, NQ // 2 - 1) as pair:
                    attend_pair(s, pair)
                attend_pair(s, NQ // 2 - 1)

            pe.wait_ge(wp_lo, 1)
            for m in range(GROUPS * NB):
                g = m // NB
                pe.wait_ge(d_lo, m + 1)
                if m >= 4:
                    pe.wait_ge(z_saved, m - 3)
                three(ps[:, m % 4], wphi[:, g], wplo[:, g], dhi[:, m % 2], dlo[:, m % 2],
                      True, True).then_inc(z_done, 1)

            def project_out(t, i):
                pe.wait_ge(c_lo, t + 1)
                if not isinstance(t, int) or t >= 2:
                    pe.wait_ge(x2_done, t - 1)
                for h in range(2):
                    for k in range(KT):
                        mm = three(ps[:, 2 * i + h], chi[:, i, k], clo[:, i, k],
                                   wohi[:, k, h * 512:(h + 1) * 512], wolo[:, k, h * 512:(h + 1) * 512],
                                   k == 0, k == KT - 1)
                mm.then_inc(out_done, 1)

            def transpose_x2(t):
                pe.wait_ge(xs2_done, t + 1)
                pe.wait_ge(h2_lo, t)
                for k in range(KT):
                    mm = pe.transpose(psw[:, 2048 + k * P:2048 + (k + 1) * P], xs2[:, k * P:(k + 1) * P], ident[:])
                mm.then_inc(xT2_done, 1)

            pe.wait_ge(wo_lo, KT)
            pe.wait_ge(z_saved, GROUPS * NB)
            project_out(0, 0)
            with pe.Fori(0, TT // 2 - 1) as h2:
                t = h2 * 2 + 1
                for i in range(2):
                    project_out(t + i, (1 + i) % 2)
                    transpose_x2(t + i - 1)
            project_out(TT - 1, 1)
            transpose_x2(TT - 2)
            transpose_x2(TT - 1)

            def up_block(c, b):
                pe.wait_ge(h2_lo, 4 * (b + 1))
                if b == 0:
                    pe.wait_ge(wu_lo, c + 1)
                for f in range(FT):
                    n = (c * NB + b) * FT + f
                    if not isinstance(n, int) or n >= 2:
                        pe.wait_ge(relu_done, n - 1)
                    for k in range(KT):
                        mm = three(ps[:, 6 + f], wuhi[:, k, f * P:(f + 1) * P], wulo[:, k, f * P:(f + 1) * P],
                                   h2hi[:, k, b * 512:(b + 1) * 512], h2lo[:, k, b * 512:(b + 1) * 512],
                                   k == 0, k == KT - 1)
                    mm.then_inc(up_done, 1)

            def down_block(c, b):
                pe.wait_ge(hid_lo_done, (c * NB + b + 1) * FT)
                if b == 0:
                    pe.wait_ge(wd_lo, c + 1)
                for t in range(4 * b, 4 * b + 4):
                    n = c * TT + t
                    if not isinstance(n, int) or n >= 3:
                        pe.wait_ge(acc_done, n - 2)
                    tok = (t % 4) * P
                    for h in range(2):
                        for f in range(FT):
                            mm = three(ps[:, 2 * (t % 3) + h],
                                       hid_hi[:, b, f, tok:tok + P], hid_lo[:, b, f, tok:tok + P],
                                       wdhi[:, f, h * 512:(h + 1) * 512], wdlo[:, f, h * 512:(h + 1) * 512],
                                       f == 0, f == FT - 1)
                    mm.then_inc(down_done, 1)

            def mlp_chunk(c):
                up_block(c, 0)
                up_block(c, 1)
                down_block(c, 0)
                up_block(c, 2)
                down_block(c, 1)
                down_block(c, 2)

            mlp_chunk(0)
            with pe.Fori(1, NCH) as c:
                mlp_chunk(c)

        @block.scalar
        def _(act):
            def copy(out, in_, **kw):
                return act.activation(out, in_, ACT.Copy, **kw)

            def square_x(t, i):
                act.wait_ge(x_in[i], 16 * (t // 2) + 16)
                act.wait_ge(msx_done, t)
                act.wait_ge(ssx_done, t)
                act.activation(junk[:], xin[:, i], ACT.Square, accum_out=ssx[:]).then_inc(ssx_done, 1)

            def split_hT(t, i):
                act.wait_ge(xT_done, t + 1)
                copy(hThi[:, i // 2, :, (i % 2) * P:(i % 2) * P + P],
                     psw[:, 0:D].rearrange("p (k c) -> p k c", k=KT)).then_inc(hT_hi, 1)

            def split_wi(k):
                act.wait_ge(w_in_in[k % 2], 16 * (k // 2 + 1))
                copy(wihi[:, k], wraw[:, k % 2]).then_inc(wi_hi, 1)

            square_x(0, 0)
            split_wi(0)
            square_x(1, 1)
            split_wi(1)
            split_hT(0, 0)
            split_wi(2)
            split_hT(1, 1)
            for k in range(3, KT):
                split_wi(k)
            square_x(2, 0)

            def project_block(n, last):
                for i in range(4):
                    t = n * 4 + i
                    act.wait_ge(qkv_done, t + 1)
                    act.wait_ge(qn_done, t)
                    copy(qk[:].rearrange("p h d -> p (h d)"), psw[:, 1024:1024 + QKW]).then_inc(qk_copied, 1)
                    copy(V[:, bass.ds(t, 1), :, 0:HEAD].rearrange("p a v d -> p (a v) d"),
                         ps[:, 3, P:2 * P].rearrange("p (v d) -> p v d", v=NKV)).then_inc(v_hi, 1)
                    act.wait_ge(qk_copied, t + 1)
                    act.wait_ge(qk_summed, t)
                    act.activation(qksq[:], qk[:], ACT.Square).then_inc(qk_squared, 1)
                    if not (last and i >= 2):
                        act.wait_ge(u_done, n * 2 + i // 2)
                        split_hT(t + 2, (i + 2) % 4)
                    if not (last and i >= 1):
                        square_x(t + 3, (i + 3) % 2)
                    if i % 2:
                        p = n * 2 + i // 2
                        act.wait_ge(u_done, p + 1)
                        copy(up[:, :, bass.ds(p * 256 + PAD + 2 * PAD * ((n + 1) // 2), 256)],
                             psw[:, 2048:3072].rearrange("p (g c) -> p g c", g=GROUPS)).then_inc(u_saved, 1)
                        for tt in (t - 1, t):
                            act.wait_ge(qkT_done, tt + 1)
                            copy(QT[:, :, bass.ds(tt * P, P)],
                                 psw[:, 3072:3072 + 5 * P].rearrange("p (j c) -> p j c", j=5)
                                 ).then_inc(qkT_saved, 1)

            with act.Fori(0, NB - 1) as n:
                project_block(n, False)
            project_block(NB - 1, True)

            act.wait_ge(qkT_saved, TT)
            act.wait_ge(u_done, TT // 2)
            for seg, (c0, n) in enumerate(SEQS):
                for kv in range(NKV):
                    for to in range(2):
                        ins = copy(KA[to * 64:to * 64 + 64, kv, c0:c0 + n], QT[kv * 64:kv * 64 + 64, 4, c0:c0 + n])
                ins.then_inc(k_hi, 1)

            def duplicate_k(seg):
                c0, n = SEQS[seg]
                act.wait_ge(k_lo, seg + 1)
                for kv in range(NKV):
                    a, b = kv * 64, (1 - kv) * 64
                    ins = copy(KB[b:b + 64, kv, c0:c0 + n], KB[a:a + 64, kv, c0:c0 + n].bitcast(F32))
                ins.then_inc(k_dup, 1)

            duplicate_k(0)
            duplicate_k(1)

            def split_q(s, pair, idx):
                j = s.job(pair, idx)
                qb, half = s.jobs[idx]
                a = half * 64
                c0 = s.start + qb * 512
                if not isinstance(j, int) or j >= 2:
                    act.wait_ge(s_done, 4 * j - 4)
                copy(Qs[a:a + 64, idx % 2], QT[a:a + 64, bass.ds(pair, 1), c0:c0 + 512]
                     .rearrange("p a c -> p (a c)")).then_inc(q_hi, 1)

            def exps(s, pair, idx, qt):
                j = s.job(pair, idx)
                act.wait_ge(max_done, 4 * j + qt + 1)
                if qt == 0:
                    if isinstance(j, int) and j == seqs[1].j0:
                        act.wait_ge(pT_done, seqs[0].tile(NQ // 2 - 1, seqs[0].per - 1, 0))
                    elif not isinstance(j, int) or j >= 2:
                        act.wait_ge(pT_done, s.tile(pair, idx - 1, 0))
                act.activation(prob[:, idx % 2, qt, 0:s.len], psw[:, (qt % 2) * 1024:(qt % 2) * 1024 + s.len],
                               ACT.Exp, bias=nmax[:, idx % 2, qt:qt + 1],
                               accum_out=rsum[:, idx % 2, qt:qt + 1]).then_inc(exp_done, 1)

            def attend_pair(s, pair):
                for idx in range(s.per):
                    j = s.job(pair, idx)
                    nxt = later_job(s, pair, idx, 1)
                    for kt in range(s.nkt):
                        act.wait_ge(pT_done, s.tile(pair, idx, kt) + 1)
                        copy(pThi[:, kt % 2], ps[:, 4 + kt % 2]).then_inc(pT_hi, 1)
                        if kt and nxt:
                            for qt in qk_slots(s).get(kt - 1, []):
                                exps(*nxt, qt)
                        if kt == s.nkt - 2 and later_job(s, pair, idx, 2):
                            split_q(*later_job(s, pair, idx, 2))
                    a, b = (0, 64) if s.jobs[idx][1] == 0 else (64, 0)
                    act.wait_ge(pv_done, s.tile(pair, idx, s.nkt - 1) + 1)
                    act.wait_ge(o_saved, j)
                    copy(half_o[a:a + 64], ps[b:b + 64, 6 + idx % 2]).then_inc(o_half, 1)

            split_q(seqs[0], 0, 0)
            split_q(seqs[0], 0, 1)
            for qt in range(4):
                exps(seqs[0], 0, 0, qt)
            for s in seqs:
                with act.Fori(0, NQ // 2 - 1) as pair:
                    attend_pair(s, pair)
                attend_pair(s, NQ // 2 - 1)

            act.wait_ge(wp_in, 16)
            copy(wphi[:], wp_raw[:]).then_inc(wp_hi, 1)

            def split_d(m):
                g, b = m // NB, m % NB
                c0 = pool_pos(min(b, 1)) + b * 512 - SEQS[min(b, 1)][0]
                if m >= 2:
                    act.wait_ge(z_done, m - 1)
                copy(dhi[:, m % 2], up[:, g, c0:c0 + 512]).then_inc(d_hi, 1)

            act.wait_ge(d_done, 2 * GROUPS)
            split_d(0)
            for m in range(GROUPS * NB):
                if m + 1 < GROUPS * NB:
                    split_d(m + 1)
                g, b = m // NB, m % NB
                act.wait_ge(z_done, m + 1)
                act.wait_ge(d_lo, m + 1)
                copy(concat[:, 4 + g, b * 512:(b + 1) * 512], ps[:, m % 4], scale=pscale[:, g:g + 1]
                     ).then_inc(z_saved, 1)
            act.wait_ge(wo_in, 16)
            act.wait_ge(pv_done, seqs[1].tile(NQ // 2, 0, 0))
            for k in range(KT):
                copy(wohi[:, k], woraw[:, k]).then_inc(wo_hi, 1)

            def split_c(t, i):
                if not isinstance(t, int) or t >= 2:
                    act.wait_ge(out_done, t - 1)
                copy(chi[:, i], concat[:, :, bass.ds(t * P, P)]).then_inc(c_hi, 1)

            def square_x2(t, i):
                act.wait_ge(x2_done, t + 1)
                act.wait_ge(ms2_done, t)
                act.wait_ge(ss2_done, t)
                act.activation(psw[:, 3072:4096], x2in[:, i], ACT.Square, accum_out=ssx[:]).then_inc(ss2_done, 1)

            def split_h2(t):
                act.wait_ge(xT2_done, t + 1)
                copy(h2hi[:, :, bass.ds(t * P, P)], psw[:, 2048:3072].rearrange("p (k c) -> p k c", k=KT)
                     ).then_inc(h2_hi, 1)

            def split_wu(c):
                act.wait_ge(wu_in, 16 * c + 16)
                act.wait_ge(up_done, FT * NB * c)
                copy(wuhi[:], wuraw[:]).then_inc(wu_hi, 1)

            act.wait_ge(z_saved, GROUPS * NB)
            act.wait_ge(o_saved, JOBS)
            split_c(0, 0)
            split_c(1, 1)
            square_x2(0, 0)
            split_wu(0)
            with act.Fori(0, TT // 2 - 1) as h2:
                t = h2 * 2 + 1
                for i in range(2):
                    split_c(t + i + 1, i % 2)
                    square_x2(t + i, (1 + i) % 2)
                    split_h2(t + i - 1)
            square_x2(TT - 1, 1)
            split_h2(TT - 2)
            split_h2(TT - 1)

            def hidden(c, b):
                for f in range(FT):
                    n = (c * NB + b) * FT + f
                    act.wait_ge(up_done, n + 1)
                    act.wait_ge(sq_done, n)
                    act.wait_ge(hid_hi_done, n)
                    act.activation(relu[:], ps[:, 6 + f], ACT.Relu).then_inc(relu_done, 1)
                    act.wait_ge(relu_done, n + 1)
                    act.activation(hid_hi[:, b, f], relu[:], ACT.Square).then_inc(hid_hi_done, 1)

            def mlp_chunk(c, last):
                hidden(c, 0)
                act.wait_ge(wd_in, 16 * c + 16)
                act.wait_ge(down_done, TT * c)
                copy(wdhi[:], wdraw[:]).then_inc(wd_hi, 1)
                hidden(c, 1)
                hidden(c, 2)
                if not last:
                    split_wu(c + 1)

            with act.Fori(0, NCH - 1) as c:
                mlp_chunk(c, False)
            mlp_chunk(NCH - 1, True)

        @block.vector
        def _(dve):
            def minus(out, a, b):
                return dve.tensor_tensor(out, a, b.bitcast(F32), ALU.subtract)

            def scale_x(t, i):
                dve.wait_ge(rsx_done, t + 1)
                dve.wait_ge(xT_done, t)
                dve.scalar_tensor_tensor(xs[:], xin[:, i], rsx[:, 0:1], g1b[:], ALU.mult, ALU.mult
                                         ).then_inc(xs_done, 1)

            def split_hT(t, i):
                dve.wait_ge(hT_hi, t + 1)
                c0 = (i % 2) * P
                minus(hTlo[:, i // 2, :, c0:c0 + P], psw[:, 0:D].rearrange("p (k c) -> p k c", k=KT),
                      hThi[:, i // 2, :, c0:c0 + P]).then_inc(hT_lo, 1)

            def split_wi(k):
                dve.wait_ge(wi_hi, k + 1)
                minus(wilo[:, k], wraw[:, k % 2], wihi[:, k]).then_inc(wi_lo, 1)

            dve.wait_ge(g1_scaled, 1)
            scale_x(0, 0)
            split_wi(0)
            scale_x(1, 1)
            split_wi(1)
            split_hT(0, 0)
            split_wi(2)
            split_hT(1, 1)
            for k in range(3, KT):
                split_wi(k)
            scale_x(2, 0)
            dve.wait_ge(gq_scaled, 1)

            def project_block(n, last):
                for i in range(4):
                    t = n * 4 + i
                    dve.wait_ge(v_hi, t + 1)
                    minus(V[:, bass.ds(t, 1), :, HEAD:].rearrange("p a v d -> p (a v) d"),
                          ps[:, 3, P:2 * P].rearrange("p (v d) -> p v d", v=NKV),
                          V[:, bass.ds(t, 1), :, 0:HEAD].rearrange("p a v d -> p (a v) d")).then_inc(v_lo, 1)
                    dve.wait_ge(qk_squared, t + 1)
                    dve.wait_ge(msqk_done, t)
                    dve.tensor_reduce(ssqk[:], qksq[:], AX.X, ALU.add).then_inc(qk_summed, 1)
                    if not (last and i >= 2):
                        split_hT(t + 2, (i + 2) % 4)
                    if not (last and i >= 1):
                        scale_x(t + 3, (i + 3) % 2)
                    dve.wait_ge(rsqk_done, t + 1)
                    dve.wait_ge(sin_done, t)
                    dve.tensor_tensor(qn[:], qk[:], rsqk[:].unsqueeze(2).to_broadcast([P, NQK, HEAD]), ALU.mult
                                      ).then_inc(qn_done, 1)
                    dve.wait_ge(qn_done, t + 1)
                    dve.tensor_tensor(qn[:], qn[:], gqkb[:], ALU.mult).then_inc(qg_done, 1)
                    dve.wait_ge(qg_done, t + 1)
                    dve.wait_ge(rope_in[i % 2], 16 * (t // 2) + 16)
                    dve.wait_ge(qkT_done, t - i % 2)
                    r = roped[:, i % 2]
                    dve.tensor_tensor(r, qn[:], rope[:, i % 2, 0].unsqueeze(1).to_broadcast([P, NQK, HEAD]),
                                      ALU.mult).then_inc(cos_done, 1)
                    dve.wait_ge(cos_done, t + 1)
                    dve.wait_ge(sin_done, t + 1)
                    dve.tensor_tensor(r, r, qsin[:], ALU.add).then_inc(rope_done, 1)

            with dve.Fori(0, NB - 1) as n:
                project_block(n, False)
            project_block(NB - 1, True)

            for seg, (c0, n) in enumerate(SEQS):
                dve.wait_ge(k_hi, seg + 1)
                for kv in range(NKV):
                    a = kv * 64
                    ins = minus(KB[a:a + 64, kv, c0:c0 + n], QT[a:a + 64, 4, c0:c0 + n], KA[a:a + 64, kv, c0:c0 + n])
                ins.then_inc(k_lo, 1)

            for s in range(2):
                for g, w in enumerate(WINDOWS):
                    dve.wait_ge(win_done, s * GROUPS + g + 1)
                    n, c0 = SEQS[s][1], pool_pos(s)
                    first = PAD - w // 2
                    dve.scalar_tensor_tensor(up[:, g, c0:c0 + n], sw[:, g % 2, first:first + n], 1.0 / w,
                                             up[:, g, c0:c0 + n], ALU.mult, ALU.subtract).then_inc(d_done, 1)

            def split_q(s, pair, idx):
                qb, half = s.jobs[idx]
                a, b = half * 64, (1 - half) * 64
                c0 = s.start + qb * 512
                dve.wait_ge(q_hi, s.job(pair, idx) + 1)
                minus(Qs[b:b + 64, idx % 2], QT[a:a + 64, bass.ds(pair, 1), c0:c0 + 512]
                      .rearrange("p a c -> p (a c)"), Qs[a:a + 64, idx % 2]).then_inc(q_lo, 1)

            def maxes(s, pair, idx, qt):
                dve.wait_ge(s_done, 4 * s.job(pair, idx) + qt + 1)
                dve.tensor_reduce(nmax[:, idx % 2, qt:qt + 1], psw[:, (qt % 2) * 1024:(qt % 2) * 1024 + s.len],
                                  AX.X, ALU.max, negate=True).then_inc(max_done, 1)

            def inverse(s, pair, idx, qt):
                dve.wait_ge(exp_done, 4 * s.job(pair, idx) + qt + 1)
                dve.reciprocal(rinv[:, idx % 2, qt:qt + 1], rsum[:, idx % 2, qt:qt + 1]).then_inc(inv_done, 1)

            def group_values(s, pair):
                dve.wait_ge(pv_done, s.tile(pair, 0, 0))
                t0 = s.start // P
                dve.tensor_copy(Vg[:, 0:s.nkt], V[:, t0:t0 + s.nkt, bass.ds(pair_kv(pair), 1), :]
                                .rearrange("p t a d -> p t (a d)").bitcast(F32)).then_inc(vg_done, 1)

            def attend_pair(s, pair):
                group_values(s, pair)
                for idx in range(s.per):
                    nxt = later_job(s, pair, idx, 1)
                    pending = []
                    for kt in range(s.nkt):
                        dve.wait_ge(pT_hi, s.tile(pair, idx, kt) + 1)
                        minus(pTlo[:, kt % 2], ps[:, 4 + kt % 2], pThi[:, kt % 2]).then_inc(pT_lo, 1)
                        for qt in pending:
                            inverse(*nxt, qt)
                        pending = []
                        if kt and nxt:
                            for qt in qk_slots(s).get(kt - 1, []):
                                maxes(*nxt, qt)
                                pending.append(qt)
                        if kt == s.nkt - 2 and later_job(s, pair, idx, 2):
                            split_q(*later_job(s, pair, idx, 2))
                    qb, half = s.jobs[idx]
                    a = half * 64
                    c0 = s.start + qb * 512
                    dve.wait_ge(o_half, s.job(pair, idx) + 1)
                    dve.tensor_tensor(concat[a:a + 64, bass.ds(pair, 1), c0:c0 + 512].rearrange("p a c -> p (a c)"),
                                      ps[a:a + 64, 6 + idx % 2], half_o[a:a + 64], ALU.add).then_inc(o_saved, 1)

            split_q(seqs[0], 0, 0)
            split_q(seqs[0], 0, 1)
            for qt in range(4):
                maxes(seqs[0], 0, 0, qt)
                inverse(seqs[0], 0, 0, qt)
            for s in seqs:
                with dve.Fori(0, NQ // 2 - 1) as pair:
                    attend_pair(s, pair)
                attend_pair(s, NQ // 2 - 1)

            dve.wait_ge(wp_hi, 1)
            minus(wplo[:], wp_raw[:], wphi[:]).then_inc(wp_lo, 1)
            for m in range(GROUPS * NB):
                g, b = m // NB, m % NB
                c0 = pool_pos(min(b, 1)) + b * 512 - SEQS[min(b, 1)][0]
                dve.wait_ge(d_hi, m + 1)
                minus(dlo[:, m % 2], up[:, g, c0:c0 + 512], dhi[:, m % 2]).then_inc(d_lo, 1)
            for k in range(KT):
                dve.wait_ge(wo_hi, k + 1)
                minus(wolo[:, k], woraw[:, k], wohi[:, k]).then_inc(wo_lo, 1)

            def split_c(t, i):
                dve.wait_ge(c_hi, t + 1)
                minus(clo[:, i], concat[:, :, bass.ds(t * P, P)], chi[:, i]).then_inc(c_lo, 1)

            def residual(t, i):
                dve.wait_ge(out_done, t + 1)
                dve.wait_ge(x2_in[i], 16 * (t // 2) + 16)
                dve.tensor_tensor(x2in[:, i], x2in[:, i], psw[:, i * 1024:(i + 1) * 1024], ALU.add
                                  ).then_inc(x2_done, 1)

            def scale_x2(t, i):
                dve.wait_ge(rs2_done, t + 1)
                dve.wait_ge(xT2_done, t)
                dve.scalar_tensor_tensor(xs2[:], x2in[:, i], rsx[:, 0:1], g2b[:], ALU.mult, ALU.mult
                                         ).then_inc(xs2_done, 1)

            def split_h2(t):
                dve.wait_ge(h2_hi, t + 1)
                minus(h2lo[:, :, bass.ds(t * P, P)], psw[:, 2048:3072].rearrange("p (k c) -> p k c", k=KT),
                      h2hi[:, :, bass.ds(t * P, P)]).then_inc(h2_lo, 1)

            def split_wu(c):
                dve.wait_ge(wu_hi, c + 1)
                minus(wulo[:], wuraw[:], wuhi[:]).then_inc(wu_lo, 1)

            split_c(0, 0)
            split_c(1, 1)
            dve.wait_ge(g2_scaled, 1)
            residual(0, 0)
            scale_x2(0, 0)
            split_wu(0)
            with dve.Fori(0, TT // 2 - 1) as h2:
                t = h2 * 2 + 1
                for i in range(2):
                    split_c(t + i + 1, i % 2)
                    residual(t + i, (1 + i) % 2)
                    split_h2(t + i - 1)
                    scale_x2(t + i, (1 + i) % 2)
            residual(TT - 1, 1)
            split_h2(TT - 2)
            scale_x2(TT - 1, 1)
            split_h2(TT - 1)

            def hidden(c, b):
                for f in range(FT):
                    n = (c * NB + b) * FT + f
                    dve.wait_ge(relu_done, n + 1)
                    dve.wait_ge(hid_lo_done, n)
                    dve.tensor_tensor(hsq[:], relu[:], relu[:], ALU.mult).then_inc(sq_done, 1)
                    dve.wait_ge(sq_done, n + 1)
                    dve.wait_ge(hid_hi_done, n + 1)
                    minus(hid_lo[:, b, f], hsq[:], hid_hi[:, b, f]).then_inc(hid_lo_done, 1)

            def accumulate(c, b):
                dve.wait_ge(y_in[b], 16)
                for t in range(4 * b, 4 * b + 4):
                    dve.wait_ge(down_done, c * TT + t + 1)
                    r = (t % 3) * 1024
                    dve.tensor_tensor(yacc[:, t], yacc[:, t], psw[:, r:r + 1024], ALU.add).then_inc(acc_done, 1)

            def mlp_chunk(c, last):
                hidden(c, 0)
                dve.wait_ge(wd_hi, c + 1)
                minus(wdlo[:], wdraw[:], wdhi[:]).then_inc(wd_lo, 1)
                hidden(c, 1)
                accumulate(c, 0)
                hidden(c, 2)
                accumulate(c, 1)
                if not last:
                    split_wu(c + 1)
                accumulate(c, 2)

            with dve.Fori(0, NCH - 1) as c:
                mlp_chunk(c, False)
            mlp_chunk(NCH - 1, True)

        @block.gpsimd
        def _(pool):
            pool.memset(mexp[:], -0.5)
            pool.memset(epsx[:], D * EPS)
            pool.memset(epsqk[:], HEAD * EPS).then_inc(mexp_set, 1)
            pool.memset(up[:], 0.0).then_inc(pads, 1)
            pool.wait_ge(mexp_set, 1)

            def rsqrt_mean(out, tmp, total, eps, started, done, n):
                pool.tensor_tensor(tmp, total, eps, ALU.add).then_inc(started, 1)
                pool.wait_ge(started, n + 1)
                pool.tensor_tensor(out, tmp, mexp[:, 0:tmp.shape[1]], ALU.pow).then_inc(done, 1)

            def norm_x(t):
                pool.wait_ge(ssx_done, t + 1)
                pool.wait_ge(xs_done, t)
                rsqrt_mean(rsx[:], msx[:], ssx[:], epsx[:], msx_done, rsx_done, t)

            pool.wait_ge(const_in, 5 * 16)
            pool.tensor_scalar(g1b[:], g1b[:], D ** 0.5, 1.0, ALU.mult, ALU.mult).then_inc(g1_scaled, 1)
            norm_x(0)
            norm_x(1)
            pool.tensor_scalar(gqkb[:, 0:NQ], gqkb[:, 0:NQ], SCALE * HEAD ** 0.5, 1.0, ALU.mult, ALU.mult)
            pool.tensor_scalar(gqkb[:, NQ:], gqkb[:, NQ:], HEAD ** 0.5, 1.0, ALU.mult, ALU.mult
                               ).then_inc(gq_scaled, 1)
            norm_x(2)

            def project_block(n, last):
                for i in range(4):
                    t = n * 4 + i
                    if not (last and i >= 1):
                        norm_x(t + 3)
                    pool.wait_ge(qk_summed, t + 1)
                    pool.wait_ge(qn_done, t)
                    rsqrt_mean(rsqk[:], msqk[:], ssqk[:], epsqk[:], msqk_done, rsqk_done, t)
                    pool.wait_ge(qg_done, t + 1)
                    pool.wait_ge(rope_in[i % 2], 16 * (t // 2) + 16)
                    pool.wait_ge(rope_done, t)
                    q4 = qn[:].rearrange("p h (a s f) -> p h a s f", a=2, s=2)
                    o4 = qsin[:].rearrange("p h (a s f) -> p h a s f", a=2, s=2)
                    sn = rope[:, i % 2, 1].rearrange("p (a s f) -> p a s f", a=2, s=2)
                    for to in range(2):
                        ins = pool.tensor_tensor(o4[:, :, :, to], q4[:, :, :, 1 - to],
                                                 sn[:, :, to].unsqueeze(1).to_broadcast([P, NQK, 2, HEAD // 4]),
                                                 ALU.mult)
                    ins.then_inc(sin_done, 1)

            with pool.Fori(0, NB - 1) as n:
                project_block(n, False)
            project_block(NB - 1, True)

            steps = 0
            pool.wait_ge(u_saved, TT // 2)
            pool.wait_ge(u_done, TT // 2)
            for s in range(2):
                n = SEQS[s][1]
                for g, w in enumerate(WINDOWS):
                    size = n + 2 * PAD
                    src = up[:, g, UP0[s]:UP0[s] + size]
                    if s or g:
                        pool.wait_ge(d_done, s * GROUPS + g)
                    for m in range(g + 1):
                        size -= 1 << m
                        if m:
                            pool.wait_ge(win_step, steps)
                        pool.tensor_tensor(sw[:, m % 2, 0:size], src[:, 0:size], src[:, 1 << m:(1 << m) + size],
                                           ALU.add).then_inc(win_step, 1)
                        steps += 1
                        src = sw[:, m % 2]
                    pool.wait_ge(win_step, steps)
                    first = PAD - w // 2
                    for e, c0 in enumerate((first, first + n - PAD)):
                        ins = pool.tensor_tensor(sw[:, g % 2, c0:c0 + PAD], sw[:, g % 2, c0:c0 + PAD],
                                                 edge[:, g, e * PAD:(e + 1) * PAD], ALU.mult)
                    ins.then_inc(win_done, 1)

            def normalize(s, pair, idx):
                for qt in range(4):
                    pool.wait_ge(inv_done, 4 * s.job(pair, idx) + qt + 1)
                    pool.tensor_tensor(rcopy[:, idx % 2, qt:qt + 1], rinv[:, idx % 2, qt:qt + 1],
                                       mexp[:, 0:1], ALU.mult).then_inc(inv_seen, 1)
                    p = prob[:, idx % 2, qt, 0:s.len]
                    pool.tensor_scalar(p, p, rinv[:, idx % 2, qt:qt + 1], 1.0, ALU.mult, ALU.mult
                                       ).then_inc(norm_done, 1)

            for s in seqs:
                with pool.Fori(0, NQ // 2) as pair:
                    for idx in range(s.per):
                        normalize(s, pair, idx)

            pool.wait_ge(g2_in, 16)
            pool.tensor_scalar(g2b[:], g2b[:], D ** 0.5, 1.0, ALU.mult, ALU.mult).then_inc(g2_scaled, 1)

            def norm_x2(t):
                pool.wait_ge(ss2_done, t + 1)
                pool.wait_ge(xs2_done, t)
                rsqrt_mean(rsx[:], msx[:], ssx[:], epsx[:], ms2_done, rs2_done, t)

            with pool.Fori(0, TT) as t:
                norm_x2(t)


def rope_tables():
    f32 = np.float32
    n_freq = HEAD // 4
    inv = (f32(THETA) ** (-np.arange(n_freq, dtype=f32) / f32(n_freq))).astype(f32)
    out = []
    for _, n in SEQS:
        pos = np.arange(n)
        ids = np.stack([pos // GRID_W, pos % GRID_W], 1).astype(f32)
        ang = (ids[:, :, None] * inv).astype(f32)
        c, s = np.cos(ang), np.sin(ang)
        out.append(np.stack([np.stack([c, c], 2).reshape(n, HEAD), np.stack([-s, s], 2).reshape(n, HEAD)], 1))
    return np.ascontiguousarray(np.concatenate(out).reshape(TT, P, 2, HEAD).astype(f32))


def edge_table():
    n = 4 * PAD
    out = np.zeros((GROUPS, 2 * PAD), np.float32)
    for g, w in enumerate(WINDOWS):
        t = np.arange(n)
        lo, hi = np.clip(t - w // 2, 0, n), np.clip(t - w // 2 + w, 0, n)
        fix = np.float32(w) / (hi - lo).astype(np.float32)
        out[g] = np.concatenate([fix[:PAD], fix[-PAD:]])
    return np.ascontiguousarray(np.broadcast_to(out, (P, GROUPS, 2 * PAD)))


def kernel(x_prompt, x_sample, norm1_g, w_in, q_norm_g, k_norm_g, w_pool, pool_scale, w_out,
           norm2_g, w_up, w_down):
    import concourse.bacc as bacc
    from concourse.bass_utils import run_bass_kernel_spmd

    a = np.asarray
    gq, gk = a(q_norm_g)[0], a(k_norm_g)[0]
    arrays = {
        "in_x": np.concatenate([a(x_prompt)[0], a(x_sample)[0]]),
        "in_g1": a(norm1_g)[0],
        "in_w_in": a(w_in)[0],
        "in_gqk": np.stack([gq] * NQ + [gk] * NKV),
        "in_w_pool": a(w_pool)[0],
        "in_pool_scale": a(pool_scale)[0].reshape(GROUPS, P).T,
        "in_w_out": a(w_out)[0],
        "in_g2": a(norm2_g)[0],
        "in_w_up": a(w_up)[0].reshape(KT, P, NCH, FC).transpose(2, 1, 0, 3),
        "in_w_down": a(w_down)[0],
        "in_ident": np.eye(P, dtype=np.float32),
        "in_rope": rope_tables(),
        "in_edge": edge_table(),
    }
    arrays = {k: np.ascontiguousarray(v) for k, v in arrays.items()}
    nc = bacc.Bacc("TRN2", target_bir_lowering=False, num_devices=1, dynamic_dma_scratch_size=512)
    args = [nc.dram_tensor(k, v.shape, mybir.dt.from_np(v.dtype), kind="ExternalInput").ap()
            for k, v in arrays.items()]
    y = nc.dram_tensor("out_y", (T, D), F32, kind="ExternalOutput").ap()
    hybrid_layer(nc, *args, y)
    r = run_bass_kernel_spmd(nc, [arrays], core_ids=[0])
    out = r.results[0]["out_y"]
    return out[None, :SEQ_P], out[None, SEQ_P:]
```

```python
from contextlib import ExitStack

import numpy as np

import concourse.bass as bass
from concourse import mybir

ALU = mybir.AluOpType
ACT = mybir.ActivationFunctionType
AX = mybir.AxisListType
F32 = mybir.dt.float32
F32R = mybir.dt.float32r

P = 128
D = 1024
KT = D // P
HEAD = 64
NQ, NKV = 8, 2
NQK = NQ + NKV
ATT = NQ * HEAD
QKW = NQK * HEAD
QKVW = ATT + 2 * NKV * HEAD
GROUPS = 4
WINDOWS = (2, 4, 8, 16)
INW = QKVW + GROUPS * P
SEQ_P, SEQ_S = 512, 1024
T = SEQ_P + SEQ_S
TT = T // P
NB = T // 512
FF = 4 * D
FC = 256
FT = FC // P
NCH = FF // FC
PAD = 8
WINDOW_STEPS = 2 * sum(g + 2 for g in range(GROUPS))
EPS = 1e-6
SCALE = HEAD ** -0.5
THETA = 10000.0
GRID_W = 64
SEQS = ((0, SEQ_P), (SEQ_P, SEQ_S))
UP0 = (0, SEQ_P + 2 * PAD)
UPW = T + 4 * PAD


def hybrid_layer(nc, x, g1, w_in, gqk, w_pool, pool_scale, w_out, g2, w_up, w_down,
                 ident_d, rope_d, edge_d, y):
    with ExitStack() as ctx:
        def sem(name):
            return ctx.enter_context(nc.semaphore(name))

        def at(name, off, shape, dt=F32):
            return nc.alloc_sbuf_tensor_at(name, [P] + shape, dt, offset=BASE + off)

        BASE = 640
        ident = at("ident", 0, [P])
        edge = at("edge", 512, [GROUPS, 2 * PAD])
        pscale = at("pscale", 768, [GROUPS])
        ssx = at("ssx", 800, [1])
        rsx = at("rsx", 832, [1])
        ssqk = at("ssqk", 864, [NQK])
        rsqk = at("rsqk", 928, [NQK])
        mexp = at("mexp", 992, [NQK])
        nmax = at("nmax", 1056, [2, 4])
        rsum = at("rsum", 1088, [2, 4])
        rinv = at("rinv", 1120, [2, 4])
        msx = at("msx", 1152, [1])
        msqk = at("msqk", 1184, [NQK])
        epsx = at("epsx", 1248, [1])
        epsqk = at("epsqk", 1280, [NQK])
        M = 1536
        X = M
        concat = at("concat", X, [KT, T])
        h2hi = at("h2hi", X, [KT, T], F32R)
        g1b = at("g1b", X, [D])
        gqkb = at("gqkb", X + 4096, [NQK, HEAD])
        rope = at("rope", X + 6656, [2, 2, HEAD])
        qn = at("qn", X + 8704, [NQK, HEAD])
        qsin = at("qsin", X + 11264, [NQK, HEAD])
        roped = at("roped", X + 13824, [2, NQK, HEAD])
        junk = at("junk", X + 18944, [D])
        up = at("up", X + 24576, [GROUPS, UPW])
        R = X + 24576 + 4 * GROUPS * UPW
        QT = at("QT", R, [5, T])
        wraw = at("wraw", R, [KT, INW])
        V = at("V", R + 30720, [TT, NKV, 2 * HEAD], F32R)
        S = R + 43008
        wihi = at("wihi", S, [KT, INW], F32R)
        wilo = at("wilo", S + 40960, [KT, INW], F32R)
        hThi = at("hThi", S + 81920, [2, KT, 256], F32R)
        hTlo = at("hTlo", S + 81920 + 16384, [2, KT, 256], F32R)
        W = S + 114688
        xin = at("xin", W, [2, D])
        xs = at("xs", W + 8192, [D])
        qk = at("qk", W + 12288, [NQK, HEAD])
        qksq = at("qksq", W + 14848, [NQK, HEAD])
        KA = at("KA", S, [NKV, T], F32R)
        KB = at("KB", S + 12288, [NKV, T], F32R)
        prob = at("prob", S + 24576, [2, 4, SEQ_S])
        pThi = at("pThi", S + 57344, [2, 512], F32R)
        pTlo = at("pTlo", S + 61440, [2, 512], F32R)
        Qs = at("Qs", S + 65536, [2, 512], F32R)
        Vg = at("Vg", S + 69632, [SEQ_S // P, 2 * HEAD], F32R)
        half_o = at("half_o", S + 73728, [512])
        sw = at("sw", S + 75776, [2, SEQ_S + 2 * PAD])
        wp_raw = at("wp_raw", S + 84224, [GROUPS, P])
        wphi = at("wphi", S + 86272, [GROUPS, P], F32R)
        wplo = at("wplo", S + 88320, [GROUPS, P], F32R)
        dhi = at("dhi", S + 90368, [2, 512], F32R)
        dlo = at("dlo", S + 94464, [2, 512], F32R)
        woraw = at("woraw", S + 98560, [KT, D])
        h2lo = at("h2lo", R, [KT, T], F32R)
        R2 = R + 49152
        wohi = at("wohi", R2, [KT, D], F32R)
        wolo = at("wolo", R2 + 32768, [KT, D], F32R)
        C = R2 + 65536
        chi = at("chi", C, [2, KT, P], F32R)
        clo = at("clo", C + 8192, [2, KT, P], F32R)
        xs2 = at("xs2", C + 16384, [D])
        g2b = at("g2b", C + 20480, [D])
        x2in = at("x2in", C + 49152, [2, D])
        yacc = at("yacc", R2, [TT, D])
        wdhi = at("wdhi", R2 + 49152, [FT, D], F32R)
        wdlo = at("wdlo", R2 + 57344, [FT, D], F32R)
        hid_hi = at("hid_hi", C, [3, FT, 512], F32R)
        hid_lo = at("hid_lo", C + 12288, [3, FT, 512], F32R)
        wuhi = at("wuhi", C + 24576, [KT, FC], F32R)
        wulo = at("wulo", C + 32768, [KT, FC], F32R)
        wuraw = at("wuraw", C + 40960, [KT, FC])
        wdraw = at("wdraw", C + 49152, [FT, D])
        relu = at("relu", C + 57344, [512])
        hsq = at("hsq", C + 59392, [512])

        ps = ctx.enter_context(nc.psum_tensor("ps", [P, 8, 512], F32))
        psw = ps[:].rearrange("p b c -> p (b c)")

        const_in = sem("const_in")
        w_in_in = [sem(f"w_in_in{k}") for k in range(KT)]
        x_in = [sem("x_in0"), sem("x_in1")]
        rope_in = [sem("rope_in0"), sem("rope_in1")]
        wi_hi = sem("wi_hi")
        wi_lo = sem("wi_lo")
        g1_scaled = sem("g1_scaled")
        g2_scaled = sem("g2_scaled")
        gq_scaled = sem("gq_scaled")
        pads = sem("pads")
        mexp_set = sem("mexp_set")
        ssx_done = sem("ssx_done")
        msx_done = sem("msx_done")
        rsx_done = sem("rsx_done")
        xs_done = sem("xs_done")
        xT_done = sem("xT_done")
        hT_hi = sem("hT_hi")
        hT_lo = sem("hT_lo")
        qkv_done = sem("qkv_done")
        u_done = sem("u_done")
        u_saved = sem("u_saved")
        qk_copied = sem("qk_copied")
        qk_squared = sem("qk_squared")
        v_hi = sem("v_hi")
        v_lo = sem("v_lo")
        qk_summed = sem("qk_summed")
        msqk_done = sem("msqk_done")
        rsqk_done = sem("rsqk_done")
        qn_done = sem("qn_done")
        qg_done = sem("qg_done")
        cos_done = sem("cos_done")
        sin_done = sem("sin_done")
        rope_done = sem("rope_done")
        qkT_done = sem("qkT_done")
        qkT_saved = sem("qkT_saved")

        win_step = sem("win_step")
        win_done = sem("win_done")
        win_edge = sem("win_edge")
        k_hi = sem("k_hi")
        k_lo = sem("k_lo")
        k_dup = [sem("k_dup0"), sem("k_dup1")]
        vg_done = sem("vg_done")
        q_hi = sem("q_hi")
        q_lo = sem("q_lo")
        s_done = sem("s_done")
        max_done = sem("max_done")
        exp_done = sem("exp_done")
        inv_done = sem("inv_done")
        norm_done = sem("norm_done")
        pT_done = sem("pT_done")
        pT_hi = sem("pT_hi")
        pT_lo = sem("pT_lo")
        pv_done = sem("pv_done")
        o_half = sem("o_half")
        o_saved = sem("o_saved")

        wp_in = sem("wp_in")
        wp_hi = sem("wp_hi")
        wp_lo = sem("wp_lo")
        d_hi = sem("d_hi")
        d_lo = sem("d_lo")
        z_done = sem("z_done")
        z_act = sem("z_act")
        z_dve = sem("z_dve")
        wo_in = sem("wo_in")
        wo_hi = sem("wo_hi")
        wo_lo = sem("wo_lo")
        g2_in = sem("g2_in")
        x2_in = [sem(f"x2_in{i}") for i in range(2)]
        c_hi = sem("c_hi")
        c_lo = sem("c_lo")
        out_done = sem("out_done")
        x2_done = sem("x2_done")
        x2_stored = [sem(f"x2_stored{i}") for i in range(2)]
        ss2_done = sem("ss2_done")
        ms2_done = sem("ms2_done")
        rs2_done = sem("rs2_done")
        xs2_done = sem("xs2_done")
        xT2_done = sem("xT2_done")
        h2_hi = sem("h2_hi")
        h2_lo = sem("h2_lo")

        y_in = [sem(f"y_in{b}") for b in range(NB)]
        wu_in = sem("wu_in")
        wd_in = sem("wd_in")
        wu_hi = sem("wu_hi")
        wu_lo = sem("wu_lo")
        wd_hi = sem("wd_hi")
        wd_lo = sem("wd_lo")
        up_done = sem("up_done")
        relu_done = sem("relu_done")
        sq_done = sem("sq_done")
        hid_hi_done = sem("hid_hi_done")
        hid_lo_done = sem("hid_lo_done")
        down_done = sem("down_done")
        acc_done = sem("acc_done")
        y_out = sem("y_out")

        block = ctx.enter_context(nc.Block())

        class Seq:
            def __init__(self, n, jobs_before, tiles_before, groups_before):
                self.n = n
                self.start, self.len = SEQS[n]
                self.nk = self.len // 512
                self.nkt = self.len // P
                self.jobs = [(qb, half) for qb in range(self.nk) for half in range(2)]
                self.per = len(self.jobs)
                self.j0 = jobs_before
                self.t0 = tiles_before
                self.group = 2 // self.nk
                self.groups = 4 // self.group
                self.g0 = groups_before

            def job(self, pair, idx):
                return self.j0 + pair * self.per + idx

            def tile(self, pair, idx, kt):
                return self.t0 + (pair * self.per + idx) * self.nkt + kt

            def score_group(self, pair, idx, u):
                return self.g0 + (pair * self.per + idx) * self.groups + u

        seqs = [Seq(0, 0, 0, 0), Seq(1, 8, 8 * (SEQ_P // P), 16)]
        JOBS = 8 + 16

        def exp_groups(s, nxt, kt):
            if not nxt or kt == 0:
                return []
            if kt < s.nkt - 1:
                return [kt - 1] if kt - 1 < nxt[0].groups else []
            return list(range(kt - 1, nxt[0].groups))

        def tight(s, nxt, kt):
            return nxt and kt == s.nkt - 1 and kt < nxt[0].groups

        def pair_kv(pair):
            return pair // (NQ // 2 // NKV)

        def later_job(s, pair, idx, ahead):
            pair, idx = pair + (idx + ahead) // s.per, (idx + ahead) % s.per
            if isinstance(pair, int) and pair >= NQ // 2:
                if s.n == 1:
                    return None
                over = (pair - NQ // 2) * s.per + idx
                return seqs[1], over // seqs[1].per, over % seqs[1].per
            return s, pair, idx

        def z_saver(m):
            return (z_act, m // 3 + 1) if m % 3 == 0 else (z_dve, m - m // 3)

        def unit_columns(m):
            g, b = m // NB, m % NB
            s = min(b, 1)
            return g, b, pool_pos(s) + b * 512 - SEQS[s][0]

        def pool_pos(s):
            return UP0[s] + PAD

        @block.sync
        def _(sp):
            sp.dma_start(xin[:, 0], x[0:P]).then_inc(x_in[0], 16)
            sp.dma_start(g1b[:], g1.partition_broadcast(P)).then_inc(const_in, 16)
            sp.dma_start(ident[:], ident_d).then_inc(const_in, 16)
            sp.dma_start(xin[:, 1], x[P:2 * P]).then_inc(x_in[1], 16)
            sp.dma_start(gqkb[:], gqk.partition_broadcast(P)).then_inc(const_in, 16)
            sp.dma_start(edge[:], edge_d).then_inc(const_in, 16)
            sp.dma_start(pscale[:], pool_scale).then_inc(const_in, 16)
            for k in range(KT):
                sp.dma_start(wraw[:, k], w_in[k * P:(k + 1) * P]).then_inc(w_in_in[k], 16)
            sp.dma_start(rope[:, 0], rope_d[0]).then_inc(rope_in[0], 16)
            sp.dma_start(rope[:, 1], rope_d[1]).then_inc(rope_in[1], 16)

            def load_x(t, i):
                sp.wait_ge(xs_done, t - 1)
                sp.dma_start(xin[:, i], x[bass.ds(t * P, P)]).then_inc(x_in[i], 16)

            def load_rope(t, i):
                sp.wait_ge(cos_done, t - 1)
                sp.wait_ge(sin_done, t - 1)
                sp.dma_start(rope[:, i], rope_d[bass.ds(t, 1)].rearrange("a p c h -> (a p) c h")
                             ).then_inc(rope_in[i], 16)

            load_x(2, 0)
            load_x(3, 1)
            with sp.Fori(2, TT // 2) as h:
                for i in range(2):
                    load_x(h * 2 + i, i)
                    load_rope(h * 2 + i - 2, i)
            load_rope(TT - 2, 0)
            load_rope(TT - 1, 1)
            sp.wait_ge(u_done, TT // 2)
            sp.wait_ge(xT_done, TT)
            sp.wait_ge(rope_done, TT)
            for seg, (c0, n) in enumerate(SEQS):
                for ready, kx in ((k_hi, KA), (k_lo, KB)):
                    sp.wait_ge(ready, seg + 1)
                    for kv in range(NKV):
                        a, b = kv * 64, (1 - kv) * 64
                        sp.dma_start(kx[b:b + 64, kv, c0:c0 + n].bitcast(F32),
                                     kx[a:a + 64, kv, c0:c0 + n].bitcast(F32)
                                     ).then_inc(k_dup[seg], 16)
            sp.dma_start(wp_raw[:], w_pool.rearrange("g c e -> c g e")).then_inc(wp_in, 16)
            sp.dma_start(woraw[:], w_out.rearrange("(k p) n -> p k n", p=P)).then_inc(wo_in, 16)
            sp.wait_ge(z_done, GROUPS * NB)
            sp.dma_start(g2b[:], g2.partition_broadcast(P)).then_inc(g2_in, 16)
            sp.wait_ge(wo_hi, KT)
            sp.wait_ge(wo_lo, KT)
            for i in range(2):
                sp.dma_start(x2in[:, i], x[i * P:(i + 1) * P]).then_inc(x2_in[i], 16)
            sp.dma_start(wuraw[:], w_up[0]).then_inc(wu_in, 16)
            with sp.Fori(0, TT // 2 - 1) as h:
                t = h * 2
                for i in range(2):
                    sp.wait_ge(x2_done, t + i + 1)
                    sp.dma_start(y[bass.ds((t + i) * P, P)], x2in[:, i]).then_inc(x2_stored[i], 16)
                for i in range(2):
                    sp.wait_ge(x2_stored[i], t * 8 + 16)
                    sp.wait_ge(xs2_done, t + i + 1)
                    sp.dma_start(x2in[:, i], x[bass.ds((t + i + 2) * P, P)]).then_inc(x2_in[i], 16)
            for i in range(2):
                sp.wait_ge(x2_done, TT - 1 + i)
                sp.dma_start(y[(TT - 2 + i) * P:(TT - 1 + i) * P], x2in[:, i]).then_inc(x2_stored[i], 16)
            sp.wait_ge(x2_stored[0], 8 * TT)
            sp.wait_ge(x2_stored[1], 8 * TT)
            sp.wait_ge(out_done, TT)
            for b in range(NB):
                sp.dma_start(yacc[:, 4 * b:4 * b + 4],
                             y[b * 512:(b + 1) * 512].rearrange("(t p) n -> p t n", p=P)).then_inc(y_in[b], 16)
            sp.wait_ge(xs2_done, TT)
            sp.dma_start(wdraw[:], w_down[0:FC].rearrange("(f p) n -> p f n", p=P)).then_inc(wd_in, 16)
            with sp.Fori(1, NCH) as c:
                sp.wait_ge(wu_hi, c)
                sp.wait_ge(wu_lo, c)
                sp.dma_start(wuraw[:], w_up[bass.ds(c, 1)].rearrange("a p k f -> (a p) k f")).then_inc(wu_in, 16)
                sp.wait_ge(wd_hi, c)
                sp.wait_ge(wd_lo, c)
                sp.dma_start(wdraw[:], w_down[bass.ds(c * FC, FC)].rearrange("(f p) n -> p f n", p=P)
                             ).then_inc(wd_in, 16)
            for b in range(NB):
                sp.wait_ge(acc_done, (NCH - 1) * TT + 4 * (b + 1))
                sp.dma_start(y[b * 512:(b + 1) * 512].rearrange("(t p) n -> p t n", p=P),
                             yacc[:, 4 * b:4 * b + 4]).then_inc(y_out, 16)
            sp.wait_ge(y_out, 16 * NB)

        @block.tensor
        def _(pe):
            def three(out, w_hi, w_lo, m_hi, m_lo, start, stop):
                pe.matmul(out, w_hi, m_hi, start=start, stop=False)
                pe.matmul(out, w_hi, m_lo, start=False, stop=False)
                return pe.matmul(out, w_lo, m_hi, start=False, stop=stop)

            def transpose_x(t):
                pe.wait_ge(xs_done, t + 1)
                pe.wait_ge(hT_lo, t)
                for k in range(KT):
                    mm = pe.transpose(psw[:, k * P:(k + 1) * P], xs[:, k * P:(k + 1) * P], ident[:])
                mm.then_inc(xT_done, 1)

            def project_qkv(t, i):
                buf, tok = i // 2, (i % 2) * P
                pe.wait_ge(hT_lo, t + 1)
                pe.wait_ge(qk_copied, t)
                pe.wait_ge(v_lo, t)
                for out, c0, c1 in ((ps[:, 2, :], 0, 512), (ps[:, 3, 0:QKVW - 512], 512, QKVW)):
                    for k in range(KT):
                        if i == 0 and c0 == 0:
                            pe.wait_ge(wi_lo, k + 1)
                        mm = three(out, hThi[:, buf, k, tok:tok + P], hTlo[:, buf, k, tok:tok + P],
                                   wihi[:, k, c0:c1], wilo[:, k, c0:c1], k == 0, k == KT - 1)
                mm.then_inc(qkv_done, 1)

            def project_u(p, buf):
                pe.wait_ge(u_saved, p)
                for g in range(GROUPS):
                    c0 = QKVW + g * P
                    for k in range(KT):
                        mm = three(ps[:, 4 + g // 2, (g % 2) * 256:(g % 2) * 256 + 256],
                                   wihi[:, k, c0:c0 + P], wilo[:, k, c0:c0 + P],
                                   hThi[:, buf, k, :], hTlo[:, buf, k, :], k == 0, k == KT - 1)
                mm.then_inc(u_done, 1)

            def transpose_qk(t, i):
                pe.wait_ge(rope_done, t + 1)
                pe.wait_ge(qkT_saved, t)
                for j in range(5):
                    mm = pe.transpose(psw[:, 3072 + j * P:3072 + (j + 1) * P],
                                      roped[:, i % 2, 2 * j:2 * j + 2].rearrange("p h d -> p (h d)"), ident[:])
                mm.then_inc(qkT_done, 1)

            def project_block(n, last):
                for i in range(4):
                    t = n * 4 + i
                    project_qkv(t, i)
                    if not (last and i >= 2):
                        transpose_x(t + 2)
                    if i % 2:
                        project_u(n * 2 + i // 2, i // 2)
                        transpose_qk(t - 1, i - 1)
                        transpose_qk(t, i)

            pe.wait_ge(const_in, 5 * 16)
            transpose_x(0)
            transpose_x(1)
            with pe.Fori(0, NB - 1) as n:
                project_block(n, False)
            project_block(NB - 1, True)

            def scores(s, pair, idx, u):
                j = s.job(pair, idx)
                if u == 0:
                    pe.wait_ge(q_lo, j + 1)
                    pe.wait_ge(k_dup[s.n], 64)
                if not isinstance(j, int) or j > 0 or u >= 2:
                    pe.wait_ge(exp_done, 4 * j + (u - 1 if s.nk == 2 else 2 * u - 2))
                kv = pair_kv(pair)
                for h in range(2):
                    qt = u * s.group + h // s.nk
                    key0 = s.start + (h % s.nk) * 512
                    out = ps[:, 2 * (u % 2) + h]
                    q = Qs[:, idx % 2, qt * P:(qt + 1) * P]
                    pe.matmul(out, q, KA[:, bass.ds(kv, 1), key0:key0 + 512].rearrange("p a c -> p (a c)"),
                              start=True, stop=False)
                    mm = pe.matmul(out, q, KB[:, bass.ds(kv, 1), key0:key0 + 512].rearrange("p a c -> p (a c)"),
                                   start=False, stop=True)
                mm.then_inc(s_done, 1)

            def transpose_p(s, pair, idx, kt):
                if kt == 0:
                    pe.wait_ge(norm_done, 4 * s.job(pair, idx) + 4)
                for qt in range(4):
                    mm = pe.transpose(ps[:, 4 + kt % 2, qt * P:(qt + 1) * P],
                                      prob[:, idx % 2, qt, kt * P:(kt + 1) * P], ident[:])
                mm.then_inc(pT_done, 1)

            def values(s, pair, idx, kt):
                pe.wait_ge(pT_lo, s.tile(pair, idx, kt) + 1)
                if kt == 0:
                    pe.wait_ge(vg_done, NQ // 2 * s.n + pair + 1)
                out = ps[:, 6 + idx % 2]
                pe.matmul(out, Vg[:, kt], pThi[:, kt % 2], start=(kt == 0), stop=False)
                pe.matmul(out, Vg[:, kt], pTlo[:, kt % 2], start=False, stop=(kt == s.nkt - 1)
                          ).then_inc(pv_done, 1)

            def attend_pair(s, pair):
                for idx in range(s.per):
                    nxt = later_job(s, pair, idx, 1)
                    for kt in range(s.nkt):
                        if kt + 1 < s.nkt:
                            transpose_p(s, pair, idx, kt + 1)
                        elif nxt and not tight(s, nxt, kt):
                            transpose_p(*nxt, 0)
                        if nxt and kt < nxt[0].groups:
                            scores(*nxt, kt)
                        values(s, pair, idx, kt)
                        if tight(s, nxt, kt):
                            transpose_p(*nxt, 0)

            for u in range(seqs[0].groups):
                scores(seqs[0], 0, 0, u)
            transpose_p(seqs[0], 0, 0, 0)
            for s in seqs:
                with pe.Fori(0, NQ // 2 - 1) as pair:
                    attend_pair(s, pair)
                attend_pair(s, NQ // 2 - 1)

            pe.wait_ge(wp_lo, 1)
            for m in range(GROUPS * NB):
                g = m // NB
                pe.wait_ge(d_lo, m + 1)
                if m >= 4:
                    pe.wait_ge(*z_saver(m - 4))
                three(ps[:, m % 4], wphi[:, g], wplo[:, g], dhi[:, m % 2], dlo[:, m % 2],
                      True, True).then_inc(z_done, 1)

            def project_out(t, i):
                pe.wait_ge(c_lo, t + 1)
                if not isinstance(t, int) or t >= 2:
                    pe.wait_ge(x2_done, t - 1)
                for h in range(2):
                    for k in range(KT):
                        mm = three(ps[:, 2 * i + h], chi[:, i, k], clo[:, i, k],
                                   wohi[:, k, h * 512:(h + 1) * 512], wolo[:, k, h * 512:(h + 1) * 512],
                                   k == 0, k == KT - 1)
                mm.then_inc(out_done, 1)

            def transpose_x2(t):
                pe.wait_ge(xs2_done, t + 1)
                pe.wait_ge(h2_lo, t)
                for k in range(KT):
                    mm = pe.transpose(psw[:, 2048 + k * P:2048 + (k + 1) * P], xs2[:, k * P:(k + 1) * P], ident[:])
                mm.then_inc(xT2_done, 1)

            pe.wait_ge(wo_lo, KT)
            project_out(0, 0)
            with pe.Fori(0, TT // 2 - 1) as h2:
                t = h2 * 2 + 1
                for i in range(2):
                    project_out(t + i, (1 + i) % 2)
                    transpose_x2(t + i - 1)
            project_out(TT - 1, 1)
            transpose_x2(TT - 2)
            transpose_x2(TT - 1)

            def up_block(c, b):
                pe.wait_ge(h2_lo, 4 * (b + 1))
                if b == 0:
                    pe.wait_ge(wu_lo, c + 1)
                for f in range(FT):
                    n = (c * NB + b) * FT + f
                    if not isinstance(n, int) or n >= 2:
                        pe.wait_ge(relu_done, n - 1)
                    for k in range(KT):
                        mm = three(ps[:, 6 + f], wuhi[:, k, f * P:(f + 1) * P], wulo[:, k, f * P:(f + 1) * P],
                                   h2hi[:, k, b * 512:(b + 1) * 512], h2lo[:, k, b * 512:(b + 1) * 512],
                                   k == 0, k == KT - 1)
                    mm.then_inc(up_done, 1)

            def down_block(c, b):
                pe.wait_ge(hid_lo_done, (c * NB + b + 1) * FT)
                if b == 0:
                    pe.wait_ge(wd_lo, c + 1)
                for t in range(4 * b, 4 * b + 4):
                    n = c * TT + t
                    if not isinstance(n, int) or n >= 3:
                        pe.wait_ge(acc_done, n - 2)
                    tok = (t % 4) * P
                    for h in range(2):
                        for f in range(FT):
                            mm = three(ps[:, 2 * (t % 3) + h],
                                       hid_hi[:, b, f, tok:tok + P], hid_lo[:, b, f, tok:tok + P],
                                       wdhi[:, f, h * 512:(h + 1) * 512], wdlo[:, f, h * 512:(h + 1) * 512],
                                       f == 0, f == FT - 1)
                    mm.then_inc(down_done, 1)

            def mlp_chunk(c):
                up_block(c, 0)
                up_block(c, 1)
                down_block(c, 0)
                up_block(c, 2)
                down_block(c, 1)
                down_block(c, 2)

            mlp_chunk(0)
            with pe.Fori(1, NCH) as c:
                mlp_chunk(c)

        @block.scalar
        def _(act):
            def copy(out, in_, **kw):
                return act.activation(out, in_, ACT.Copy, **kw)

            def square_x(t, i):
                act.wait_ge(x_in[i], 16 * (t // 2) + 16)
                act.wait_ge(msx_done, t)
                act.wait_ge(ssx_done, t)
                act.activation(junk[:], xin[:, i], ACT.Square, accum_out=ssx[:]).then_inc(ssx_done, 1)

            def split_hT(t, i):
                act.wait_ge(xT_done, t + 1)
                copy(hThi[:, i // 2, :, (i % 2) * P:(i % 2) * P + P],
                     psw[:, 0:D].rearrange("p (k c) -> p k c", k=KT)).then_inc(hT_hi, 1)

            def split_wi(k):
                act.wait_ge(w_in_in[k], 16)
                copy(wihi[:, k], wraw[:, k]).then_inc(wi_hi, 1)

            square_x(0, 0)
            split_wi(0)
            square_x(1, 1)
            split_wi(1)
            split_hT(0, 0)
            split_wi(2)
            split_hT(1, 1)
            for k in range(3, KT):
                split_wi(k)
            square_x(2, 0)

            def project_block(n, last):
                for i in range(4):
                    t = n * 4 + i
                    act.wait_ge(qkv_done, t + 1)
                    act.wait_ge(qn_done, t)
                    copy(qk[:].rearrange("p h d -> p (h d)"), psw[:, 1024:1024 + QKW]).then_inc(qk_copied, 1)
                    copy(V[:, bass.ds(t, 1), :, 0:HEAD].rearrange("p a v d -> p (a v) d"),
                         ps[:, 3, P:2 * P].rearrange("p (v d) -> p v d", v=NKV)).then_inc(v_hi, 1)
                    act.wait_ge(qk_copied, t + 1)
                    act.wait_ge(qk_summed, t)
                    act.activation(qksq[:], qk[:], ACT.Square).then_inc(qk_squared, 1)
                    if not (last and i >= 2):
                        act.wait_ge(u_done, n * 2 + i // 2)
                        split_hT(t + 2, (i + 2) % 4)
                    if not (last and i >= 1):
                        square_x(t + 3, (i + 3) % 2)
                    if i % 2:
                        p = n * 2 + i // 2
                        act.wait_ge(u_done, p + 1)
                        copy(up[:, :, bass.ds(p * 256 + PAD + 2 * PAD * ((n + 1) // 2), 256)],
                             psw[:, 2048:3072].rearrange("p (g c) -> p g c", g=GROUPS)).then_inc(u_saved, 1)
                        for tt in (t - 1, t):
                            act.wait_ge(qkT_done, tt + 1)
                            copy(QT[:, :, bass.ds(tt * P, P)],
                                 psw[:, 3072:3072 + 5 * P].rearrange("p (j c) -> p j c", j=5)
                                 ).then_inc(qkT_saved, 1)

            with act.Fori(0, NB - 1) as n:
                project_block(n, False)
            project_block(NB - 1, True)

            def split_k(seg):
                c0, n = SEQS[seg]
                for kv in range(NKV):
                    a = kv * 64
                    ins = copy(KA[a:a + 64, kv, c0:c0 + n], QT[a:a + 64, 4, c0:c0 + n])
                ins.then_inc(k_hi, 1)

            act.wait_ge(qkT_saved, TT)
            act.wait_ge(u_done, TT // 2)
            split_k(0)

            def split_q(s, pair, idx):
                j = s.job(pair, idx)
                qb, half = s.jobs[idx]
                a = half * 64
                c0 = s.start + qb * 512
                if isinstance(j, int) and j == seqs[1].j0:
                    act.wait_ge(s_done, seqs[0].score_group(0, j - 1, 0))
                elif not isinstance(j, int) or j >= 2:
                    act.wait_ge(s_done, s.score_group(pair, idx - 1, 0))
                copy(Qs[a:a + 64, idx % 2], QT[a:a + 64, bass.ds(pair, 1), c0:c0 + 512]
                     .rearrange("p a c -> p (a c)")).then_inc(q_hi, 1)

            def exps(s, pair, idx, u):
                act.wait_ge(max_done, s.score_group(pair, idx, u) + 1)
                for qt in range(u * s.group, (u + 1) * s.group):
                    c0 = (u % 2) * 1024 + (qt % s.group) * 512
                    act.activation(prob[:, idx % 2, qt, 0:s.len], psw[:, c0:c0 + s.len],
                                   ACT.Exp, bias=nmax[:, idx % 2, qt:qt + 1],
                                   accum_out=rsum[:, idx % 2, qt:qt + 1]).then_inc(exp_done, 1)

            def split_p(s, pair, idx, kt):
                act.wait_ge(pT_done, s.tile(pair, idx, kt) + 1)
                copy(pThi[:, kt % 2], ps[:, 4 + kt % 2]).then_inc(pT_hi, 1)

            def attend_pair(s, pair):
                for idx in range(s.per):
                    j = s.job(pair, idx)
                    nxt = later_job(s, pair, idx, 1)
                    for kt in range(s.nkt):
                        if kt + 1 < s.nkt:
                            split_p(s, pair, idx, kt + 1)
                        elif nxt and not tight(s, nxt, kt):
                            split_p(*nxt, 0)
                        for u in exp_groups(s, nxt, kt):
                            exps(*nxt, u)
                        if tight(s, nxt, kt):
                            split_p(*nxt, 0)
                        if kt == s.nkt - 2 and later_job(s, pair, idx, 2):
                            split_q(*later_job(s, pair, idx, 2))
                    a, b = (0, 64) if s.jobs[idx][1] == 0 else (64, 0)
                    act.wait_ge(pv_done, s.tile(pair, idx, s.nkt - 1) + 1)
                    act.wait_ge(o_saved, j)
                    copy(half_o[a:a + 64], ps[b:b + 64, 6 + idx % 2]).then_inc(o_half, 1)

            split_q(seqs[0], 0, 0)
            split_q(seqs[0], 0, 1)
            for u in range(seqs[0].groups):
                exps(seqs[0], 0, 0, u)
            split_k(1)
            split_p(seqs[0], 0, 0, 0)
            for s in seqs:
                with act.Fori(0, NQ // 2 - 1) as pair:
                    attend_pair(s, pair)
                attend_pair(s, NQ // 2 - 1)

            act.wait_ge(wp_in, 16)
            copy(wphi[:], wp_raw[:]).then_inc(wp_hi, 1)

            def split_d(m):
                g, b, c0 = unit_columns(m)
                if m >= 2:
                    act.wait_ge(z_done, m - 1)
                copy(dhi[:, m % 2], up[:, g, c0:c0 + 512]).then_inc(d_hi, 1)

            act.wait_ge(win_step, WINDOW_STEPS)
            act.wait_ge(pv_done, seqs[1].tile(NQ // 2, 0, 0))
            act.wait_ge(wo_in, 16)
            split_d(0)
            for m in range(GROUPS * NB):
                if m + 1 < GROUPS * NB:
                    split_d(m + 1)
                if m < KT:
                    copy(wohi[:, m], woraw[:, m]).then_inc(wo_hi, 1)
                if m % 3 == 0:
                    g, b, _ = unit_columns(m)
                    act.wait_ge(z_done, m + 1)
                    copy(concat[:, 4 + g, b * 512:(b + 1) * 512], ps[:, m % 4], scale=pscale[:, g:g + 1]
                         ).then_inc(z_act, 1)

            def split_c(t, i):
                if not isinstance(t, int) or t >= 2:
                    act.wait_ge(out_done, t - 1)
                copy(chi[:, i], concat[:, :, bass.ds(t * P, P)]).then_inc(c_hi, 1)

            def square_x2(t, i):
                act.wait_ge(x2_done, t + 1)
                act.wait_ge(ms2_done, t)
                act.wait_ge(ss2_done, t)
                act.activation(psw[:, 3072:4096], x2in[:, i], ACT.Square, accum_out=ssx[:]).then_inc(ss2_done, 1)

            def split_h2(t):
                act.wait_ge(xT2_done, t + 1)
                copy(h2hi[:, :, bass.ds(t * P, P)], psw[:, 2048:3072].rearrange("p (k c) -> p k c", k=KT)
                     ).then_inc(h2_hi, 1)

            def split_wu(c):
                act.wait_ge(wu_in, 16 * c + 16)
                act.wait_ge(up_done, FT * NB * c)
                copy(wuhi[:], wuraw[:]).then_inc(wu_hi, 1)

            act.wait_ge(z_dve, GROUPS * NB - GROUPS)
            act.wait_ge(z_act, GROUPS)
            act.wait_ge(o_saved, JOBS)
            split_c(0, 0)
            split_c(1, 1)
            square_x2(0, 0)
            split_wu(0)
            with act.Fori(0, TT // 2 - 1) as h2:
                t = h2 * 2 + 1
                for i in range(2):
                    split_c(t + i + 1, i % 2)
                    square_x2(t + i, (1 + i) % 2)
                    split_h2(t + i - 1)
            square_x2(TT - 1, 1)
            split_h2(TT - 2)
            split_h2(TT - 1)

            def hidden(c, b):
                for f in range(FT):
                    n = (c * NB + b) * FT + f
                    act.wait_ge(up_done, n + 1)
                    act.wait_ge(sq_done, n)
                    act.wait_ge(hid_hi_done, n)
                    act.activation(relu[:], ps[:, 6 + f], ACT.Relu).then_inc(relu_done, 1)
                    act.wait_ge(relu_done, n + 1)
                    act.activation(hid_hi[:, b, f], relu[:], ACT.Square).then_inc(hid_hi_done, 1)

            def mlp_chunk(c, last):
                hidden(c, 0)
                act.wait_ge(wd_in, 16 * c + 16)
                act.wait_ge(down_done, TT * c)
                copy(wdhi[:], wdraw[:]).then_inc(wd_hi, 1)
                hidden(c, 1)
                hidden(c, 2)
                if not last:
                    split_wu(c + 1)

            with act.Fori(0, NCH - 1) as c:
                mlp_chunk(c, False)
            mlp_chunk(NCH - 1, True)

        @block.vector
        def _(dve):
            def minus(out, a, b):
                return dve.tensor_tensor(out, a, b.bitcast(F32), ALU.subtract)

            def scale_x(t, i):
                dve.wait_ge(rsx_done, t + 1)
                dve.wait_ge(xT_done, t)
                dve.scalar_tensor_tensor(xs[:], xin[:, i], rsx[:, 0:1], g1b[:], ALU.mult, ALU.mult
                                         ).then_inc(xs_done, 1)

            def split_hT(t, i):
                dve.wait_ge(hT_hi, t + 1)
                c0 = (i % 2) * P
                minus(hTlo[:, i // 2, :, c0:c0 + P], psw[:, 0:D].rearrange("p (k c) -> p k c", k=KT),
                      hThi[:, i // 2, :, c0:c0 + P]).then_inc(hT_lo, 1)

            def split_wi(k):
                dve.wait_ge(wi_hi, k + 1)
                minus(wilo[:, k], wraw[:, k], wihi[:, k]).then_inc(wi_lo, 1)

            dve.wait_ge(g1_scaled, 1)
            scale_x(0, 0)
            split_wi(0)
            scale_x(1, 1)
            split_wi(1)
            split_hT(0, 0)
            split_wi(2)
            split_hT(1, 1)
            for k in range(3, KT):
                split_wi(k)
            scale_x(2, 0)
            dve.wait_ge(gq_scaled, 1)

            def project_block(n, last):
                for i in range(4):
                    t = n * 4 + i
                    dve.wait_ge(v_hi, t + 1)
                    minus(V[:, bass.ds(t, 1), :, HEAD:].rearrange("p a v d -> p (a v) d"),
                          ps[:, 3, P:2 * P].rearrange("p (v d) -> p v d", v=NKV),
                          V[:, bass.ds(t, 1), :, 0:HEAD].rearrange("p a v d -> p (a v) d")).then_inc(v_lo, 1)
                    dve.wait_ge(qk_squared, t + 1)
                    dve.wait_ge(msqk_done, t)
                    dve.tensor_reduce(ssqk[:], qksq[:], AX.X, ALU.add).then_inc(qk_summed, 1)
                    if not (last and i >= 2):
                        split_hT(t + 2, (i + 2) % 4)
                    if not (last and i >= 1):
                        scale_x(t + 3, (i + 3) % 2)
                    dve.wait_ge(rsqk_done, t + 1)
                    dve.wait_ge(sin_done, t)
                    dve.tensor_tensor(qn[:], qk[:], rsqk[:].unsqueeze(2).to_broadcast([P, NQK, HEAD]), ALU.mult
                                      ).then_inc(qn_done, 1)
                    dve.wait_ge(qn_done, t + 1)
                    dve.tensor_tensor(qn[:], qn[:], gqkb[:], ALU.mult).then_inc(qg_done, 1)
                    dve.wait_ge(qg_done, t + 1)
                    dve.wait_ge(rope_in[i % 2], 16 * (t // 2) + 16)
                    dve.wait_ge(qkT_done, t - i % 2)
                    r = roped[:, i % 2]
                    dve.tensor_tensor(r, qn[:], rope[:, i % 2, 0].unsqueeze(1).to_broadcast([P, NQK, HEAD]),
                                      ALU.mult).then_inc(cos_done, 1)
                    dve.wait_ge(cos_done, t + 1)
                    dve.wait_ge(sin_done, t + 1)
                    dve.tensor_tensor(r, r, qsin[:], ALU.add).then_inc(rope_done, 1)

            with dve.Fori(0, NB - 1) as n:
                project_block(n, False)
            project_block(NB - 1, True)

            def split_k(seg):
                c0, n = SEQS[seg]
                dve.wait_ge(k_hi, seg + 1)
                for kv in range(NKV):
                    a = kv * 64
                    ins = minus(KB[a:a + 64, kv, c0:c0 + n], QT[a:a + 64, 4, c0:c0 + n], KA[a:a + 64, kv, c0:c0 + n])
                ins.then_inc(k_lo, 1)

            split_k(0)

            def split_q(s, pair, idx):
                qb, half = s.jobs[idx]
                a, b = half * 64, (1 - half) * 64
                c0 = s.start + qb * 512
                dve.wait_ge(q_hi, s.job(pair, idx) + 1)
                minus(Qs[b:b + 64, idx % 2], QT[a:a + 64, bass.ds(pair, 1), c0:c0 + 512]
                      .rearrange("p a c -> p (a c)"), Qs[a:a + 64, idx % 2]).then_inc(q_lo, 1)

            def maxes(s, pair, idx, u):
                dve.wait_ge(s_done, s.score_group(pair, idx, u) + 1)
                dve.tensor_reduce(nmax[:, idx % 2, u * s.group:(u + 1) * s.group],
                                  psw[:, (u % 2) * 1024:(u % 2) * 1024 + 1024].rearrange("p (q c) -> p q c", c=s.len),
                                  AX.X, ALU.max, negate=True).then_inc(max_done, 1)

            def inverses(s, pair, idx, u):
                q0, q1 = u * s.group, (u + 1) * s.group
                dve.wait_ge(exp_done, 4 * s.job(pair, idx) + q1)
                dve.reciprocal(rinv[:, idx % 2, q0:q1], rsum[:, idx % 2, q0:q1]).then_inc(inv_done, 1)

            def group_values(s, pair):
                if not isinstance(pair, int) or pair or s.n:
                    dve.wait_ge(pv_done, s.tile(pair, 0, 0))
                t0 = s.start // P
                dve.tensor_copy(Vg[:, 0:s.nkt], V[:, t0:t0 + s.nkt, bass.ds(pair_kv(pair), 1), :]
                                .rearrange("p t a d -> p t (a d)").bitcast(F32)).then_inc(vg_done, 1)

            def split_p(s, pair, idx, kt):
                dve.wait_ge(pT_hi, s.tile(pair, idx, kt) + 1)
                minus(pTlo[:, kt % 2], ps[:, 4 + kt % 2], pThi[:, kt % 2]).then_inc(pT_lo, 1)

            def attend_pair(s, pair):
                for idx in range(s.per):
                    nxt = later_job(s, pair, idx, 1)
                    for kt in range(s.nkt):
                        if kt + 1 < s.nkt:
                            split_p(s, pair, idx, kt + 1)
                        elif nxt and not tight(s, nxt, kt):
                            split_p(*nxt, 0)
                        if nxt and kt < nxt[0].groups:
                            maxes(*nxt, kt)
                        for u in exp_groups(s, nxt, kt):
                            inverses(*nxt, u)
                        if tight(s, nxt, kt):
                            split_p(*nxt, 0)
                        if kt == s.nkt - 2 and later_job(s, pair, idx, 2):
                            split_q(*later_job(s, pair, idx, 2))
                    qb, half = s.jobs[idx]
                    a = half * 64
                    c0 = s.start + qb * 512
                    dve.wait_ge(o_half, s.job(pair, idx) + 1)
                    dve.tensor_tensor(concat[a:a + 64, bass.ds(pair, 1), c0:c0 + 512].rearrange("p a c -> p (a c)"),
                                      ps[a:a + 64, 6 + idx % 2], half_o[a:a + 64], ALU.add).then_inc(o_saved, 1)
                nxt = later_job(s, pair, s.per - 1, 1)
                if nxt:
                    group_values(nxt[0], nxt[1])

            group_values(seqs[0], 0)
            split_q(seqs[0], 0, 0)
            split_q(seqs[0], 0, 1)
            for u in range(seqs[0].groups):
                maxes(seqs[0], 0, 0, u)
                inverses(seqs[0], 0, 0, u)
            split_k(1)
            split_p(seqs[0], 0, 0, 0)
            for s in seqs:
                with dve.Fori(0, NQ // 2 - 1) as pair:
                    attend_pair(s, pair)
                attend_pair(s, NQ // 2 - 1)

            dve.wait_ge(wp_hi, 1)
            minus(wplo[:], wp_raw[:], wphi[:]).then_inc(wp_lo, 1)
            for m in range(GROUPS * NB):
                if m < KT:
                    dve.wait_ge(wo_hi, m + 1)
                    minus(wolo[:, m], woraw[:, m], wohi[:, m]).then_inc(wo_lo, 1)
                if m % 3:
                    g, b, _ = unit_columns(m)
                    dve.wait_ge(z_done, m + 1)
                    dve.tensor_scalar(concat[:, 4 + g, b * 512:(b + 1) * 512], ps[:, m % 4],
                                      pscale[:, g:g + 1], None, ALU.mult).then_inc(z_dve, 1)

            def split_c(t, i):
                dve.wait_ge(c_hi, t + 1)
                minus(clo[:, i], concat[:, :, bass.ds(t * P, P)], chi[:, i]).then_inc(c_lo, 1)

            def residual(t, i):
                dve.wait_ge(out_done, t + 1)
                dve.wait_ge(x2_in[i], 16 * (t // 2) + 16)
                dve.tensor_tensor(x2in[:, i], x2in[:, i], psw[:, i * 1024:(i + 1) * 1024], ALU.add
                                  ).then_inc(x2_done, 1)

            def scale_x2(t, i):
                dve.wait_ge(rs2_done, t + 1)
                dve.wait_ge(xT2_done, t)
                dve.scalar_tensor_tensor(xs2[:], x2in[:, i], rsx[:, 0:1], g2b[:], ALU.mult, ALU.mult
                                         ).then_inc(xs2_done, 1)

            def split_h2(t):
                dve.wait_ge(h2_hi, t + 1)
                minus(h2lo[:, :, bass.ds(t * P, P)], psw[:, 2048:3072].rearrange("p (k c) -> p k c", k=KT),
                      h2hi[:, :, bass.ds(t * P, P)]).then_inc(h2_lo, 1)

            def split_wu(c):
                dve.wait_ge(wu_hi, c + 1)
                minus(wulo[:], wuraw[:], wuhi[:]).then_inc(wu_lo, 1)

            split_c(0, 0)
            split_c(1, 1)
            dve.wait_ge(g2_scaled, 1)
            residual(0, 0)
            scale_x2(0, 0)
            split_wu(0)
            with dve.Fori(0, TT // 2 - 1) as h2:
                t = h2 * 2 + 1
                for i in range(2):
                    split_c(t + i + 1, i % 2)
                    residual(t + i, (1 + i) % 2)
                    split_h2(t + i - 1)
                    scale_x2(t + i, (1 + i) % 2)
            residual(TT - 1, 1)
            split_h2(TT - 2)
            scale_x2(TT - 1, 1)
            split_h2(TT - 1)

            def hidden(c, b):
                for f in range(FT):
                    n = (c * NB + b) * FT + f
                    dve.wait_ge(relu_done, n + 1)
                    dve.wait_ge(hid_lo_done, n)
                    dve.tensor_tensor(hsq[:], relu[:], relu[:], ALU.mult).then_inc(sq_done, 1)
                    dve.wait_ge(sq_done, n + 1)
                    dve.wait_ge(hid_hi_done, n + 1)
                    minus(hid_lo[:, b, f], hsq[:], hid_hi[:, b, f]).then_inc(hid_lo_done, 1)

            def accumulate(c, b):
                dve.wait_ge(y_in[b], 16)
                for t in range(4 * b, 4 * b + 4):
                    dve.wait_ge(down_done, c * TT + t + 1)
                    r = (t % 3) * 1024
                    dve.tensor_tensor(yacc[:, t], yacc[:, t], psw[:, r:r + 1024], ALU.add).then_inc(acc_done, 1)

            def mlp_chunk(c, last):
                hidden(c, 0)
                dve.wait_ge(wd_hi, c + 1)
                minus(wdlo[:], wdraw[:], wdhi[:]).then_inc(wd_lo, 1)
                hidden(c, 1)
                accumulate(c, 0)
                hidden(c, 2)
                accumulate(c, 1)
                if not last:
                    split_wu(c + 1)
                accumulate(c, 2)

            with dve.Fori(0, NCH - 1) as c:
                mlp_chunk(c, False)
            mlp_chunk(NCH - 1, True)

        @block.gpsimd
        def _(pool):
            pool.memset(mexp[:], -0.5)
            pool.memset(epsx[:], D * EPS)
            pool.memset(epsqk[:], HEAD * EPS).then_inc(mexp_set, 1)
            pool.memset(up[:], 0.0).then_inc(pads, 1)
            pool.wait_ge(mexp_set, 1)

            def rsqrt_mean(out, tmp, total, eps, started, done, n):
                pool.tensor_tensor(tmp, total, eps, ALU.add).then_inc(started, 1)
                pool.wait_ge(started, n + 1)
                pool.tensor_tensor(out, tmp, mexp[:, 0:tmp.shape[1]], ALU.pow).then_inc(done, 1)

            def norm_x(t):
                pool.wait_ge(ssx_done, t + 1)
                pool.wait_ge(xs_done, t)
                rsqrt_mean(rsx[:], msx[:], ssx[:], epsx[:], msx_done, rsx_done, t)

            pool.wait_ge(const_in, 5 * 16)
            pool.tensor_scalar(g1b[:], g1b[:], D ** 0.5, 1.0, ALU.mult, ALU.mult).then_inc(g1_scaled, 1)
            norm_x(0)
            norm_x(1)
            pool.tensor_scalar(gqkb[:, 0:NQ], gqkb[:, 0:NQ], SCALE * HEAD ** 0.5, 1.0, ALU.mult, ALU.mult)
            pool.tensor_scalar(gqkb[:, NQ:], gqkb[:, NQ:], HEAD ** 0.5, 1.0, ALU.mult, ALU.mult
                               ).then_inc(gq_scaled, 1)
            norm_x(2)

            def project_block(n, last):
                for i in range(4):
                    t = n * 4 + i
                    if not (last and i >= 1):
                        norm_x(t + 3)
                    pool.wait_ge(qk_summed, t + 1)
                    pool.wait_ge(qn_done, t)
                    rsqrt_mean(rsqk[:], msqk[:], ssqk[:], epsqk[:], msqk_done, rsqk_done, t)
                    pool.wait_ge(qg_done, t + 1)
                    pool.wait_ge(rope_in[i % 2], 16 * (t // 2) + 16)
                    pool.wait_ge(rope_done, t)
                    q4 = qn[:].rearrange("p h (a s f) -> p h a s f", a=2, s=2)
                    o4 = qsin[:].rearrange("p h (a s f) -> p h a s f", a=2, s=2)
                    sn = rope[:, i % 2, 1].rearrange("p (a s f) -> p a s f", a=2, s=2)
                    for to in range(2):
                        ins = pool.tensor_tensor(o4[:, :, :, to], q4[:, :, :, 1 - to],
                                                 sn[:, :, to].unsqueeze(1).to_broadcast([P, NQK, 2, HEAD // 4]),
                                                 ALU.mult)
                    ins.then_inc(sin_done, 1)

            with pool.Fori(0, NB - 1) as n:
                project_block(n, False)
            project_block(NB - 1, True)

            steps = [(s, g, m) for s in range(2) for g in range(GROUPS) for m in range(g + 2)]

            def window_step(k):
                s, g, m = steps[k]
                n, w = SEQS[s][1], WINDOWS[g]
                if k:
                    pool.wait_ge(win_step, k)
                if m <= g:
                    size = n + 2 * PAD - (2 << m) + 1
                    src = up[:, g, UP0[s]:UP0[s] + n + 2 * PAD] if m == 0 else sw[:, (m + 1) % 2]
                    pool.tensor_tensor(sw[:, m % 2, 0:size], src[:, 0:size], src[:, 1 << m:(1 << m) + size],
                                       ALU.add).then_inc(win_step, 1)
                    return
                first = PAD - w // 2
                sums = sw[:, g % 2, first:first + n]
                for e, part in enumerate((sums[:, 0:PAD], sums[:, n - PAD:n])):
                    ins = pool.tensor_tensor(part, part, edge[:, g, e * PAD:(e + 1) * PAD], ALU.mult)
                ins.then_inc(win_edge, 1)
                pool.wait_ge(win_edge, s * GROUPS + g + 1)
                pool.tensor_scalar(sums, sums, 1.0 / w, 1.0, ALU.mult, ALU.mult).then_inc(win_done, 1)
                pool.wait_ge(win_done, s * GROUPS + g + 1)
                c0 = pool_pos(s)
                pool.tensor_tensor(up[:, g, c0:c0 + n], sums, up[:, g, c0:c0 + n], ALU.subtract
                                   ).then_inc(win_step, 1)

            assert len(steps) == WINDOW_STEPS
            half = len(steps) // 2
            pool.wait_ge(u_saved, TT // 2)
            pool.wait_ge(u_done, TT // 2)
            step, invs = 0, 0
            for s in seqs:
                for pair in range(NQ // 2):
                    for idx in range(s.per):
                        for qt in range(4):
                            if qt % s.group == 0:
                                invs += 1
                            pool.wait_ge(inv_done, invs)
                            p = prob[:, idx % 2, qt, 0:s.len]
                            pool.tensor_scalar(p, p, rinv[:, idx % 2, qt:qt + 1], 1.0, ALU.mult, ALU.mult
                                               ).then_inc(norm_done, 1)
                        for _ in range(2 if step < half else 1):
                            if step < len(steps):
                                window_step(step)
                                step += 1

            for m in range(GROUPS * NB):
                g, b, c0 = unit_columns(m)
                pool.wait_ge(d_hi, m + 1)
                pool.tensor_tensor(dlo[:, m % 2], up[:, g, c0:c0 + 512], dhi[:, m % 2].bitcast(F32),
                                   ALU.subtract).then_inc(d_lo, 1)

            def norm_x2(t):
                pool.wait_ge(ss2_done, t + 1)
                pool.wait_ge(xs2_done, t)
                rsqrt_mean(rsx[:], msx[:], ssx[:], epsx[:], ms2_done, rs2_done, t)

            pool.wait_ge(g2_in, 16)
            pool.tensor_scalar(g2b[:], g2b[:], D ** 0.5, 1.0, ALU.mult, ALU.mult).then_inc(g2_scaled, 1)
            with pool.Fori(0, TT) as t:
                norm_x2(t)


def rope_tables():
    f32 = np.float32
    n_freq = HEAD // 4
    inv = (f32(THETA) ** (-np.arange(n_freq, dtype=f32) / f32(n_freq))).astype(f32)
    out = []
    for _, n in SEQS:
        pos = np.arange(n)
        ids = np.stack([pos // GRID_W, pos % GRID_W], 1).astype(f32)
        ang = (ids[:, :, None] * inv).astype(f32)
        c, s = np.cos(ang), np.sin(ang)
        out.append(np.stack([np.stack([c, c], 2).reshape(n, HEAD), np.stack([-s, s], 2).reshape(n, HEAD)], 1))
    return np.ascontiguousarray(np.concatenate(out).reshape(TT, P, 2, HEAD).astype(f32))


def edge_table():
    n = 4 * PAD
    out = np.zeros((GROUPS, 2 * PAD), np.float32)
    for g, w in enumerate(WINDOWS):
        t = np.arange(n)
        lo, hi = np.clip(t - w // 2, 0, n), np.clip(t - w // 2 + w, 0, n)
        fix = np.float32(w) / (hi - lo).astype(np.float32)
        out[g] = np.concatenate([fix[:PAD], fix[-PAD:]])
    return np.ascontiguousarray(np.broadcast_to(out, (P, GROUPS, 2 * PAD)))


def kernel(x_prompt, x_sample, norm1_g, w_in, q_norm_g, k_norm_g, w_pool, pool_scale, w_out,
           norm2_g, w_up, w_down):
    import concourse.bacc as bacc
    from concourse.bass_utils import run_bass_kernel_spmd

    a = np.asarray
    gq, gk = a(q_norm_g)[0], a(k_norm_g)[0]
    arrays = {
        "in_x": np.concatenate([a(x_prompt)[0], a(x_sample)[0]]),
        "in_g1": a(norm1_g)[0],
        "in_w_in": a(w_in)[0],
        "in_gqk": np.stack([gq] * NQ + [gk] * NKV),
        "in_w_pool": a(w_pool)[0],
        "in_pool_scale": a(pool_scale)[0].reshape(GROUPS, P).T,
        "in_w_out": a(w_out)[0],
        "in_g2": a(norm2_g)[0],
        "in_w_up": a(w_up)[0].reshape(KT, P, NCH, FC).transpose(2, 1, 0, 3),
        "in_w_down": a(w_down)[0],
        "in_ident": np.eye(P, dtype=np.float32),
        "in_rope": rope_tables(),
        "in_edge": edge_table(),
    }
    arrays = {k: np.ascontiguousarray(v) for k, v in arrays.items()}
    nc = bacc.Bacc("TRN2", target_bir_lowering=False, num_devices=1, dynamic_dma_scratch_size=512)
    args = [nc.dram_tensor(k, v.shape, mybir.dt.from_np(v.dtype), kind="ExternalInput").ap()
            for k, v in arrays.items()]
    y = nc.dram_tensor("out_y", (T, D), F32, kind="ExternalOutput").ap()
    hybrid_layer(nc, *args, y)
    r = run_bass_kernel_spmd(nc, [arrays], core_ids=[0])
    out = r.results[0]["out_y"]
    return out[None, :SEQ_P], out[None, SEQ_P:]
```

```python
from contextlib import ExitStack

import numpy as np

import concourse.bass as bass
from concourse import mybir

ALU = mybir.AluOpType
ACT = mybir.ActivationFunctionType
AX = mybir.AxisListType
F32 = mybir.dt.float32
F32R = mybir.dt.float32r

P = 128
D = 1024
KT = D // P
HEAD = 64
NQ, NKV = 8, 2
NQK = NQ + NKV
ATT = NQ * HEAD
QKW = NQK * HEAD
QKVW = ATT + 2 * NKV * HEAD
GROUPS = 4
WINDOWS = (2, 4, 8, 16)
INW = QKVW + GROUPS * P
SEQ_P, SEQ_S = 512, 1024
T = SEQ_P + SEQ_S
TT = T // P
NB = T // 512
FF = 4 * D
FC = 256
FT = FC // P
NCH = FF // FC
PAD = 8
WINDOW_STEPS = 2 * sum(g + 2 for g in range(GROUPS))
EPS = 1e-6
SCALE = HEAD ** -0.5
THETA = 10000.0
GRID_W = 64
SEQS = ((0, SEQ_P), (SEQ_P, SEQ_S))
UP0 = (0, SEQ_P + 2 * PAD)
UPW = T + 4 * PAD


def hybrid_layer(nc, x, g1, w_in, gqk, w_pool, pool_scale, w_out, g2, w_up, w_down,
                 ident_d, rope_d, edge_d, y):
    with ExitStack() as ctx:
        def sem(name):
            return ctx.enter_context(nc.semaphore(name))

        def at(name, off, shape, dt=F32):
            return nc.alloc_sbuf_tensor_at(name, [P] + shape, dt, offset=BASE + off)

        BASE = 640
        ident = at("ident", 0, [P])
        edge = at("edge", 512, [GROUPS, 2 * PAD])
        pscale = at("pscale", 768, [GROUPS])
        ssx = at("ssx", 800, [1])
        rsx = at("rsx", 832, [1])
        ssqk = at("ssqk", 864, [NQK])
        rsqk = at("rsqk", 928, [NQK])
        mexp = at("mexp", 992, [NQK])
        nmax = at("nmax", 1344, [2, 8])
        rsum = at("rsum", 1408, [2, 8])
        rinv = at("rinv", 1472, [2, 8])
        msx = at("msx", 1152, [1])
        msqk = at("msqk", 1184, [NQK])
        epsx = at("epsx", 1248, [1])
        epsqk = at("epsqk", 1280, [NQK])
        M = 1536
        X = M
        concat = at("concat", X, [KT, T])
        h2hi = at("h2hi", X, [KT, T], F32R)
        g1b = at("g1b", X, [D])
        gqkb = at("gqkb", X + 4096, [NQK, HEAD])
        rope = at("rope", X + 6656, [2, 2, HEAD])
        qn = at("qn", X + 8704, [NQK, HEAD])
        qsin = at("qsin", X + 11264, [NQK, HEAD])
        roped = at("roped", X + 13824, [2, NQK, HEAD])
        junk = at("junk", X + 18944, [D])
        up = at("up", X + 24576, [GROUPS, UPW])
        R = X + 24576 + 4 * GROUPS * UPW
        QT = at("QT", R, [5, T])
        wraw = at("wraw", R, [KT, INW])
        V = at("V", R + 30720, [TT, NKV, 2 * HEAD], F32R)
        S = R + 43008
        wihi = at("wihi", S, [KT, INW], F32R)
        wilo = at("wilo", S + 40960, [KT, INW], F32R)
        hThi = [at(f"hThi{i}", S + 81920 + i * 16384, [KT, 256], F32R) for i in range(2)]
        hTlo = [at(f"hTlo{i}", S + 90112 + i * 16384, [KT, 256], F32R) for i in range(2)]
        W = S + 114688
        xin = at("xin", W, [2, D])
        xs = at("xs", W + 8192, [D])
        qk = at("qk", W + 12288, [NQK, HEAD])
        qksq = at("qksq", W + 14848, [NQK, HEAD])
        KA = [at("KA0", X + 20480, [NKV, SEQ_P], F32R), at("KA1", S + 6144, [NKV, SEQ_S], F32R)]
        KB = [at("KB0", W, [NKV, SEQ_P], F32R), at("KB1", S + 14336, [NKV, SEQ_S], F32R)]
        Qs = at("Qs", W + 4096, [4, 512], F32R)
        prob = [at("prob0", S + 81920, [4, 1024]), at("prob1", S + 38912, [4, 1024])]
        pThi = at("pThi", S + 55296, [4, 512], F32R)
        pTlo = at("pTlo", S + 63488, [4, 512], F32R)
        Vg = at("Vg", S + 71680, [SEQ_S // P, 2 * HEAD], F32R)
        o_full = at("o_full", S, [2, 512])
        o_part = at("o_part", S + 4096, [512])
        sw_sample = [at(f"sw_sample{i}", S + 22528 + i * 4160, [SEQ_S + 2 * PAD]) for i in range(2)]
        sw_prompt = [at("sw_prompt0", X, [SEQ_P + 2 * PAD]), at("sw_prompt1", W + 17408, [SEQ_P + 2 * PAD])]
        woraw = at("woraw", S + 98304, [KT, D])
        wp_raw = at("wp_raw", S + 131072, [GROUPS, P])
        dhi = at("dhi", R, [4, 512], F32R)
        dlo = at("dlo", R + 8192, [4, 512], F32R)
        wphi = at("wphi", R + 16384, [GROUPS, P], F32R)
        wplo = at("wplo", R + 18432, [GROUPS, P], F32R)
        h2lo = at("h2lo", R, [KT, T], F32R)
        R2 = R + 49152
        wohi = at("wohi", R2, [KT, D], F32R)
        wolo = at("wolo", R2 + 32768, [KT, D], F32R)
        C = R2 + 65536
        chi = at("chi", C, [2, KT, P], F32R)
        clo = at("clo", C + 8192, [2, KT, P], F32R)
        junk2 = at("junk2", C + 57344, [D])
        xs2 = at("xs2", C + 16384, [D])
        g2b = at("g2b", C + 20480, [D])
        x2in = at("x2in", C + 49152, [2, D])
        yacc = at("yacc", R2, [TT, D])
        wdhi = at("wdhi", R2 + 49152, [FT, D], F32R)
        wdlo = at("wdlo", R2 + 57344, [FT, D], F32R)
        hid_hi = at("hid_hi", C, [3, FT, 512], F32R)
        hid_lo = at("hid_lo", C + 12288, [3, FT, 512], F32R)
        wuhi = at("wuhi", C + 24576, [KT, FC], F32R)
        wulo = at("wulo", C + 32768, [KT, FC], F32R)
        wuraw = at("wuraw", C + 40960, [KT, FC])
        wdraw = at("wdraw", C + 49152, [FT, D])
        relu = at("relu", C + 57344, [512])
        hsq = at("hsq", C + 59392, [512])

        ps = ctx.enter_context(nc.psum_tensor("ps", [P, 8, 512], F32))
        psw = ps[:].rearrange("p b c -> p (b c)")

        ident_in = sem("ident_in")
        g1_in = sem("g1_in")
        gqk_in = sem("gqk_in")
        pool_in = sem("pool_in")
        w_in_in = [sem(f"w_in_in{k}") for k in range(KT)]
        x_in = [sem("x_in0"), sem("x_in1")]
        rope_in = [sem("rope_in0"), sem("rope_in1")]
        w_u_in = [sem("w_u_in0"), sem("w_u_in1")]
        wi_hi = sem("wi_hi")
        wi_lo = sem("wi_lo")
        wi_u_hi = sem("wi_u_hi")
        wi_u_lo = sem("wi_u_lo")
        gq_scaled = sem("gq_scaled")
        pads = sem("pads")
        mexp_set = sem("mexp_set")
        ssx_done = sem("ssx_done")
        msx_done = sem("msx_done")
        rsx_done = sem("rsx_done")
        xs_done = sem("xs_done")
        xT_done = sem("xT_done")
        hT_hi = sem("hT_hi")
        hT_lo = sem("hT_lo")
        qkv_done = sem("qkv_done")
        u_done = sem("u_done")
        u_saved = sem("u_saved")
        qk_copied = sem("qk_copied")
        qk_squared = sem("qk_squared")
        v_hi = sem("v_hi")
        v_lo = sem("v_lo")
        qk_summed = sem("qk_summed")
        msqk_done = sem("msqk_done")
        rsqk_done = sem("rsqk_done")
        qn_done = sem("qn_done")
        qg_done = sem("qg_done")
        cos_done = sem("cos_done")
        sin_done = sem("sin_done")
        rope_done = sem("rope_done")
        qkT_done = sem("qkT_done")
        qkT_saved = sem("qkT_saved")

        win_step = sem("win_step")
        win_done = sem("win_done")
        win_edge = sem("win_edge")
        k_hi = sem("k_hi")
        k_lo = sem("k_lo")
        k_dup = [sem("k_dup0"), sem("k_dup1")]
        vg_done = sem("vg_done")
        q_hi = sem("q_hi")
        q_lo = [sem("q_lo_prompt"), sem("q_lo_sample")]
        s_done = sem("s_done")
        max_done = sem("max_done")
        exp_done = sem("exp_done")
        inv_done = sem("inv_done")
        norm_done = sem("norm_done")
        pT_done = sem("pT_done")
        pT_hi = sem("pT_hi")
        pT_lo = sem("pT_lo")
        pv_done = sem("pv_done")
        o_copied = sem("o_copied")
        o_moved = [sem("o_moved0"), sem("o_moved1")]
        o_saved = sem("o_saved")

        wp_in = sem("wp_in")
        wp_hi = sem("wp_hi")
        wp_lo = sem("wp_lo")
        d_hi = sem("d_hi")
        d_lo = sem("d_lo")
        z_done = sem("z_done")
        z_act = sem("z_act")
        z_dve = sem("z_dve")
        wo_in = [sem("wo_in0"), sem("wo_in1")]
        wo_hi = sem("wo_hi")
        wo_lo = sem("wo_lo")
        g2_in = sem("g2_in")
        x2_in = [sem(f"x2_in{i}") for i in range(2)]
        c_hi = sem("c_hi")
        c_lo = sem("c_lo")
        out_done = sem("out_done")
        x2_done = sem("x2_done")
        x2_stored = [sem(f"x2_stored{i}") for i in range(2)]
        ss2_done = sem("ss2_done")
        ms2_done = sem("ms2_done")
        rs2_done = sem("rs2_done")
        xs2_done = sem("xs2_done")
        xT2_done = sem("xT2_done")
        h2_hi = sem("h2_hi")
        h2_lo = sem("h2_lo")

        y_in = [sem(f"y_in{b}") for b in range(NB)]
        wu_in = sem("wu_in")
        wd_in = sem("wd_in")
        wu_hi = sem("wu_hi")
        wu_lo = sem("wu_lo")
        wd_hi = sem("wd_hi")
        wd_lo = sem("wd_lo")
        up_done = sem("up_done")
        relu_done = sem("relu_done")
        sq_done = sem("sq_done")
        hid_hi_done = sem("hid_hi_done")
        hid_lo_done = sem("hid_lo_done")
        down_done = sem("down_done")
        acc_done = sem("acc_done")
        y_out = sem("y_out")

        FIRST = 1
        block = ctx.enter_context(nc.Block())

        STEPS, GRP = 8, 4

        class Seq:
            def __init__(self, n):
                self.n = n
                self.start, self.len = SEQS[n]
                self.per = 1 if n == 0 else 4
                self.tiles = 1024 // self.len
                self.halves = 2 if n == 0 else 1
                self.kts = self.len // P

            def job(self, pair, idx):
                return NQ // 2 * self.n + pair * self.per + idx

            def turn(self, pair, idx, k):
                return self.job(pair, idx) * STEPS + k

            def group(self, pair, idx, u):
                return self.job(pair, idx) * GRP + u

            def out(self, pair, idx, half):
                return NQ * self.n + pair * self.per * self.halves + idx + half * (self.n == 0)

            def parity(self, pair, idx):
                return (idx if self.n else pair) % 2

            def half_of(self, idx, k):
                return idx % 2 if self.n else k // self.kts

        seqs = [Seq(0), Seq(1)]
        OUTS = NQ + 2 * NQ
        JOBS = seqs[1].job(NQ // 2, 0)
        GROUPS_ALL = seqs[1].group(NQ // 2, 0, 0)

        def pair_kv(pair):
            return pair // (NQ // 2 // NKV)

        def later_job(s, pair, idx, ahead):
            pair, idx = pair + (idx + ahead) // s.per, (idx + ahead) % s.per
            if isinstance(pair, int) and pair >= NQ // 2:
                if s.n == 1:
                    return None
                over = (pair - NQ // 2) * s.per + idx
                return seqs[1], over // seqs[1].per, over % seqs[1].per
            return s, pair, idx

        def scored_in(s, pair, idx, k):
            if k % 2 == 0:
                return None
            later = later_job(s, pair, idx, 1 if k == 1 else 2)
            return later and (*later, (k // 2 + 3) % GRP)

        def transposed_in(s, pair, idx, k):
            if k + 2 < STEPS:
                return s, pair, idx, k + 2
            later = later_job(s, pair, idx, 1)
            return later and (*later, k + 2 - STEPS)

        def exped_in(s, pair, idx, k):
            if k % 2 == 0:
                return None
            later = later_job(s, pair, idx, 1 if k < 4 else 2)
            return later and (*later, (k // 2 + 2) % GRP)

        def inverted_in(s, pair, idx, k):
            if k % 2:
                return None
            if k:
                return exped_in(s, pair, idx, k - 1)
            later = later_job(s, pair, idx, 1)
            return later and (*later, 1)

        def q_split_in(s, pair, idx, k):
            later = later_job(s, pair, idx, 3)
            if not later:
                return None
            if later[0].n:
                return (*later, 0) if k == 4 else None
            return (*later, (k - 4) // 2) if k in (4, 6) else None

        def z_saver(m):
            return (z_act, m // 3 + 1) if m % 3 == 0 else (z_dve, m - m // 3)

        def unit_columns(m):
            g, b = m // NB, m % NB
            s = min(b, 1)
            return g, b, pool_pos(s) + b * 512 - SEQS[s][0]

        def pool_pos(s):
            return UP0[s] + PAD

        @block.sync
        def _(sp):
            def load_x(t, i):
                sp.wait_ge(xs_done, t - 1)
                sp.dma_start(xin[:, i], x[bass.ds(t * P, P)]).then_inc(x_in[i], 16)

            sp.dma_start(xin[:, 0], x[0:P]).then_inc(x_in[0], 16)
            sp.dma_start(g1b[:], g1.partition_broadcast(P)).then_inc(g1_in, 16)
            sp.dma_start(ident[:], ident_d).then_inc(ident_in, 16)
            sp.dma_start(wraw[:, 0, 0:QKVW], w_in[0:P, 0:QKVW]).then_inc(w_in_in[0], 16)
            sp.dma_start(xin[:, 1], x[P:2 * P]).then_inc(x_in[1], 16)
            for k in range(1, KT):
                sp.dma_start(wraw[:, k, 0:QKVW], w_in[k * P:(k + 1) * P, 0:QKVW]).then_inc(w_in_in[k], 16)
                if k == 4:
                    load_x(2, 0)
            for k in (0, KT // 2):
                sp.dma_start(wraw[:, k:k + KT // 2, QKVW:],
                             w_in[k * P:(k + KT // 2) * P, QKVW:].rearrange("(k p) n -> p k n", p=P)
                             ).then_inc(w_u_in[k // (KT // 2)], 16)
            load_x(3, 1)
            sp.dma_start(gqkb[:], gqk.partition_broadcast(P)).then_inc(gqk_in, 16)
            sp.dma_start(rope[:, 0], rope_d[0]).then_inc(rope_in[0], 16)
            sp.dma_start(rope[:, 1], rope_d[1]).then_inc(rope_in[1], 16)
            sp.dma_start(edge[:], edge_d).then_inc(pool_in, 16)
            sp.dma_start(pscale[:], pool_scale).then_inc(pool_in, 16)

            def load_rope(t, i):
                sp.wait_ge(cos_done, FIRST + t - 1)
                sp.wait_ge(sin_done, FIRST + t - 1)
                sp.dma_start(rope[:, i], rope_d[bass.ds(t, 1)].rearrange("a p c h -> (a p) c h")
                             ).then_inc(rope_in[i], 16)

            with sp.Fori(2, TT // 2) as h:
                for i in range(2):
                    load_x(h * 2 + i, i)
                    load_rope(h * 2 + i - 2, i)
            load_rope(TT - 2, 0)
            load_rope(TT - 1, 1)
            def double_k(seg, kv):
                a, b = kv * 64, (1 - kv) * 64
                for ready, kx in ((k_hi, KA[seg]), (k_lo, KB[seg])):
                    sp.wait_ge(ready, seg * NKV + kv + 1)
                    sp.dma_start(kx[b:b + 64, kv].bitcast(F32), kx[a:a + 64, kv].bitcast(F32)
                                 ).then_inc(k_dup[seg], 16)

            double_k(0, 0)
            double_k(0, 1)
            sp.wait_ge(u_done, FIRST + TT // 2)
            sp.wait_ge(qkT_saved, FIRST + TT)
            wo = w_out.rearrange("(k p) n -> p k n", p=P)
            sp.wait_ge(win_step, WINDOW_STEPS // 2)
            sp.dma_start(wp_raw[:], w_pool.rearrange("g c e -> c g e")).then_inc(wp_in, 16)
            sp.dma_start(woraw[:, 0:4], wo[:, 0:4]).then_inc(wo_in[0], 16)

            def move_out(s, pair, idx, half):
                n = s.out(pair, idx, half)
                a, b = half * 64, (1 - half) * 64
                sp.wait_ge(o_copied, n + 1)
                sp.dma_start(o_part[a:a + 64], o_full[b:b + 64, half]).then_inc(o_moved[half], 16)

            for pair in range(NQ // 2):
                if pair < NKV:
                    double_k(1, pair)
                for half in range(2):
                    move_out(seqs[0], pair, 0, half)
            with sp.Fori(0, NQ // 2 - 1) as pair:
                for idx in range(4):
                    move_out(seqs[1], pair, idx, idx % 2)
            for idx in range(4):
                if idx == 2:
                    sp.wait_ge(s_done, seqs[1].group(NQ // 2, 0, 0))
                    sp.dma_start(woraw[:, 4:], wo[:, 4:]).then_inc(wo_in[1], 16)
                move_out(seqs[1], NQ // 2 - 1, idx, idx % 2)
            sp.dma_start(g2b[:], g2.partition_broadcast(P)).then_inc(g2_in, 16)
            sp.wait_ge(wo_hi, KT)
            sp.wait_ge(wo_lo, KT)
            for i in range(2):
                sp.dma_start(x2in[:, i], x[i * P:(i + 1) * P]).then_inc(x2_in[i], 16)
            sp.dma_start(wuraw[:], w_up[0]).then_inc(wu_in, 16)
            with sp.Fori(0, TT // 2 - 1) as h:
                t = h * 2
                for i in range(2):
                    sp.wait_ge(x2_done, FIRST + t + i + 1)
                    sp.dma_start(y[bass.ds((t + i) * P, P)], x2in[:, i]).then_inc(x2_stored[i], 16)
                for i in range(2):
                    sp.wait_ge(x2_stored[i], t * 8 + 16)
                    sp.wait_ge(xs2_done, FIRST + t + i + 1)
                    sp.dma_start(x2in[:, i], x[bass.ds((t + i + 2) * P, P)]).then_inc(x2_in[i], 16)
            for i in range(2):
                sp.wait_ge(x2_done, FIRST + TT - 1 + i)
                sp.dma_start(y[(TT - 2 + i) * P:(TT - 1 + i) * P], x2in[:, i]).then_inc(x2_stored[i], 16)
            def reload(b):
                sp.dma_start(yacc[:, 4 * b:4 * b + 4],
                             y[b * 512:(b + 1) * 512].rearrange("(t p) n -> p t n", p=P)).then_inc(y_in[b], 16)

            sp.wait_ge(out_done, TT)
            reload(0)
            sp.wait_ge(xs2_done, FIRST + TT)
            sp.wait_ge(x2_stored[0], 8 * TT)
            sp.wait_ge(x2_stored[1], 8 * TT)
            sp.dma_start(wdraw[:], w_down[0:FC].rearrange("(f p) n -> p f n", p=P)).then_inc(wd_in, 16)
            reload(1)
            reload(2)
            with sp.Fori(1, NCH) as c:
                sp.wait_ge(wu_hi, c)
                sp.wait_ge(wu_lo, c)
                sp.dma_start(wuraw[:], w_up[bass.ds(c, 1)].rearrange("a p k f -> (a p) k f")).then_inc(wu_in, 16)
                sp.wait_ge(wd_hi, c)
                sp.wait_ge(wd_lo, c)
                sp.dma_start(wdraw[:], w_down[bass.ds(c * FC, FC)].rearrange("(f p) n -> p f n", p=P)
                             ).then_inc(wd_in, 16)
            for b in range(NB - 1):
                sp.wait_ge(acc_done, (NCH - 1) * TT + 4 * (b + 1))
                sp.dma_start(y[b * 512:(b + 1) * 512].rearrange("(t p) n -> p t n", p=P),
                             yacc[:, 4 * b:4 * b + 4]).then_inc(y_out, 16)
            for t in range(TT - 4, TT):
                sp.wait_ge(acc_done, (NCH - 1) * TT + t + 1)
                sp.dma_start(y[t * P:(t + 1) * P], yacc[:, t]).then_inc(y_out, 16)
            sp.wait_ge(y_out, 16 * (NB - 1 + 4))

        @block.tensor
        def _(pe):
            for count in (u_done, down_done, qkT_done):
                pe.sem_inc(count, FIRST)

            def three(out, w_hi, w_lo, m_hi, m_lo, start, stop):
                pe.matmul(out, w_hi, m_hi, start=start, stop=False)
                pe.matmul(out, w_hi, m_lo, start=False, stop=False)
                return pe.matmul(out, w_lo, m_hi, start=False, stop=stop)

            def transpose_x(t):
                pe.wait_ge(xs_done, t + 1)
                pe.wait_ge(hT_lo, t)
                for k in range(KT):
                    mm = pe.transpose(psw[:, k * P:(k + 1) * P], xs[:, k * P:(k + 1) * P], ident[:])
                mm.then_inc(xT_done, 1)

            def project_qkv(t, i):
                buf, tok = i // 2, (i % 2) * P
                pe.wait_ge(hT_lo, t + 1)
                pe.wait_ge(qk_copied, FIRST + t)
                for out, c0, c1 in ((ps[:, 2, :], 0, 512), (ps[:, 3, 0:QKVW - 512], 512, QKVW)):
                    if c0:
                        pe.wait_ge(v_lo, FIRST + t)
                    for k in range(KT):
                        if i == 0 and c0 == 0:
                            pe.wait_ge(wi_lo, k + 1)
                        mm = three(out, hThi[buf][:, k, tok:tok + P], hTlo[buf][:, k, tok:tok + P],
                                   wihi[:, k, c0:c1], wilo[:, k, c0:c1], k == 0, k == KT - 1)
                mm.then_inc(qkv_done, 1)

            def project_u(p, buf, between):
                pe.wait_ge(u_saved, FIRST + p)
                pe.wait_ge(wi_u_lo, KT)
                for g in range(GROUPS):
                    between(g)
                    c0 = QKVW + g * P
                    for k in range(KT):
                        mm = three(ps[:, 4 + g // 2, (g % 2) * 256:(g % 2) * 256 + 256],
                                   wihi[:, k, c0:c0 + P], wilo[:, k, c0:c0 + P],
                                   hThi[buf][:, k, :], hTlo[buf][:, k, :], k == 0, k == KT - 1)
                mm.then_inc(u_done, 1)

            def transpose_qk(t, i):
                pe.wait_ge(rope_done, FIRST + t + 1)
                pe.wait_ge(qkT_saved, FIRST + t)
                for j in range(5):
                    mm = pe.transpose(psw[:, 3072 + j * P:3072 + (j + 1) * P],
                                      roped[:, i % 2, 2 * j:2 * j + 2].rearrange("p h d -> p (h d)"), ident[:])
                mm.then_inc(qkT_done, 1)

            def project_block(n, last):
                for i in range(4):
                    t = n * 4 + i
                    project_qkv(t, i)
                    if not (last and i >= 2):
                        transpose_x(t + 2)
                    if i % 2:
                        def between(g):
                            if g == 2:
                                transpose_qk(t - 1, i - 1)
                            if last and i == 3:
                                first_scores(g)
                        project_u(n * 2 + i // 2, i // 2, between)
                        transpose_qk(t, i)

            def scores(s, pair, idx, u):
                g = s.group(pair, idx, u)
                half = u // 2 if s.n == 0 else 0
                if u % (GRP // s.halves) == 0:
                    pe.wait_ge(q_lo[s.n], s.out(pair, idx, half) - NQ * s.n + 1)
                pe.wait_ge(k_dup[s.n], 64)
                if not isinstance(g, int) or g >= 2:
                    pe.wait_ge(exp_done, g - 1)
                kv = pair_kv(pair)
                for h in range(2):
                    qt = u if s.n else 2 * (u % 2) + h
                    key0 = h * 512 * s.n
                    out = ps[:, 2 * (u % 2) + h]
                    q = Qs[:, 2 * s.parity(pair, idx) + half, qt * P:(qt + 1) * P]
                    pe.matmul(out, q, KA[s.n][:, bass.ds(kv, 1), key0:key0 + 512].rearrange("p a c -> p (a c)"),
                              start=True, stop=False)
                    mm = pe.matmul(out, q, KB[s.n][:, bass.ds(kv, 1), key0:key0 + 512].rearrange("p a c -> p (a c)"),
                                   start=False, stop=True)
                mm.then_inc(s_done, 1)

            def transpose_p(s, pair, idx, k):
                half = s.half_of(idx, k) if s.n == 0 else 0
                if k % s.kts == 0:
                    pe.wait_ge(norm_done, s.group(pair, idx, (half + 1) * GRP // s.halves))
                if k < 2 and not (s.n == 0 and pair == 0):
                    pe.wait_ge(pT_lo, s.turn(pair, idx, k) - 1)
                for qt in range(4):
                    u, c0 = (qt, 0) if s.n else (2 * half + qt // 2, (qt % 2) * 512)
                    c0 += (k % s.kts) * P
                    mm = pe.transpose(ps[:, 4 + k % 3, qt * P:(qt + 1) * P],
                                      prob[s.parity(pair, idx)][:, u, c0:c0 + P], ident[:])
                mm.then_inc(pT_done, 1)

            def values(s, pair, idx, k):
                kt = k % s.kts
                if kt == 0:
                    n = s.out(pair, idx, s.half_of(idx, k) if s.n == 0 else 0)
                    if not isinstance(n, int) or n > 0:
                        pe.wait_ge(o_copied, n)
                if s.n and idx == 0 and k % 4 == 0:
                    pe.wait_ge(vg_done, 2 * pair + 1 + k // 4)
                pe.wait_ge(pT_lo, s.turn(pair, idx, k) + 1)
                v = Vg[:, kt] if s.n else V[:, kt, pair_kv(pair)]
                pe.matmul(ps[:, 7], v, pThi[:, k % 4], start=(kt == 0), stop=False)
                pe.matmul(ps[:, 7], v, pTlo[:, k % 4], start=False, stop=(kt == s.kts - 1)
                          ).then_inc(pv_done, 1)

            def map_pool(m):
                if m == 0:
                    pe.wait_ge(wp_lo, 1)
                    pe.wait_ge(exp_done, GROUPS_ALL)
                g, b, _ = unit_columns(m)
                pe.wait_ge(d_lo, m + 1)
                if m >= 4:
                    pe.wait_ge(*z_saver(m - 4))
                three(ps[:, m % 4], wphi[:, g], wplo[:, g], dhi[:, m % 4], dlo[:, m % 4],
                      True, True).then_inc(z_done, 1)

            def attend(s, pair, last=False):
                for idx in range(s.per):
                    for k in range(STEPS):
                        if transposed_in(s, pair, idx, k):
                            transpose_p(*transposed_in(s, pair, idx, k))
                        ends = (k + 1) % s.kts == 0
                        if ends:
                            values(s, pair, idx, k)
                        if scored_in(s, pair, idx, k):
                            scores(*scored_in(s, pair, idx, k))
                        if not ends:
                            values(s, pair, idx, k)
                        if last and idx == 3:
                            if k == 0:
                                map_pool(0)
                            map_pool(k + 1)

            def first_scores(u):
                if u == 0:
                    pe.wait_ge(hT_lo, TT)
                if u == 1:
                    pe.wait_ge(qk_copied, FIRST + TT)
                    pe.wait_ge(v_lo, FIRST + TT)
                scores(seqs[0], 0, 0, u)

            pe.wait_ge(ident_in, 16)
            transpose_x(0)
            transpose_x(1)
            with pe.Fori(0, NB - 1) as n:
                project_block(n, False)
            project_block(NB - 1, True)

            scores(seqs[0], 1, 0, 0)
            pe.wait_ge(u_saved, FIRST + TT // 2)
            pe.wait_ge(qkT_saved, FIRST + TT)
            transpose_p(seqs[0], 0, 0, 0)
            scores(seqs[0], 1, 0, 1)
            transpose_p(seqs[0], 0, 0, 1)
            scores(seqs[0], 1, 0, 2)
            for pair in range(NQ // 2):
                attend(seqs[0], pair)
            with pe.Fori(0, NQ // 2 - 1) as pair:
                attend(seqs[1], pair)
            attend(seqs[1], NQ // 2 - 1, True)

            for m in range(9, GROUPS * NB):
                map_pool(m)

            def project_out(t, i):
                pe.wait_ge(c_lo, t + 1)
                if not isinstance(t, int) or t >= 2:
                    pe.wait_ge(x2_done, FIRST + t - 1)
                for k in range(KT):
                    if isinstance(t, int) and t == 0:
                        pe.wait_ge(wo_hi, k + 1)
                    for c in (chi, clo):
                        for h in range(2):
                            pe.matmul(ps[:, 2 * i + h], c[:, i, k], wohi[:, k, h * 512:(h + 1) * 512],
                                      start=(k == 0 and c is chi), stop=False)
                for k in range(KT):
                    if isinstance(t, int) and t == 0:
                        pe.wait_ge(wo_lo, k + 1)
                    for h in range(2):
                        mm = pe.matmul(ps[:, 2 * i + h], chi[:, i, k], wolo[:, k, h * 512:(h + 1) * 512],
                                       start=False, stop=(k == KT - 1))
                mm.then_inc(out_done, 1)

            def transpose_x2(t):
                pe.wait_ge(xs2_done, FIRST + t + 1)
                pe.wait_ge(h2_lo, FIRST + t)
                for k in range(KT):
                    mm = pe.transpose(psw[:, 2048 + k * P:2048 + (k + 1) * P], xs2[:, k * P:(k + 1) * P], ident[:])
                mm.then_inc(xT2_done, 1)

            project_out(0, 0)
            with pe.Fori(0, TT // 2 - 1) as h2:
                t = h2 * 2 + 1
                for i in range(2):
                    project_out(t + i, (1 + i) % 2)
                    transpose_x2(t + i - 1)
            project_out(TT - 1, 1)
            transpose_x2(TT - 2)

            def up_block(c, b, between=None):
                pe.wait_ge(h2_lo, FIRST + 4 * (b + 1))
                if b == 0:
                    pe.wait_ge(wu_lo, c + 1)
                for f in range(FT):
                    n = (c * NB + b) * FT + f
                    if not isinstance(n, int) or n >= 2:
                        pe.wait_ge(relu_done, n - 1)
                    for k in range(KT):
                        mm = three(ps[:, 6 + f], wuhi[:, k, f * P:(f + 1) * P], wulo[:, k, f * P:(f + 1) * P],
                                   h2hi[:, k, b * 512:(b + 1) * 512], h2lo[:, k, b * 512:(b + 1) * 512],
                                   k == 0, k == KT - 1)
                    mm.then_inc(up_done, 1)
                    if between and f == 0:
                        between()

            def down_block(c, b):
                pe.wait_ge(hid_lo_done, FIRST + (c * NB + b + 1) * FT)
                if b == 0:
                    pe.wait_ge(wd_lo, c + 1)
                for t in range(4 * b, 4 * b + 4):
                    n = c * TT + t
                    if not isinstance(n, int) or n >= 3:
                        pe.wait_ge(acc_done, n - 2)
                    tok = (t % 4) * P
                    for h in range(2):
                        for f in range(FT):
                            mm = three(ps[:, 2 * (t % 3) + h],
                                       hid_hi[:, b, f, tok:tok + P], hid_lo[:, b, f, tok:tok + P],
                                       wdhi[:, f, h * 512:(h + 1) * 512], wdlo[:, f, h * 512:(h + 1) * 512],
                                       f == 0, f == FT - 1)
                    mm.then_inc(down_done, 1)

            def mlp_chunk(c, between=None):
                up_block(c, 0, between)
                up_block(c, 1)
                down_block(c, 0)
                up_block(c, 2)
                down_block(c, 1)
                down_block(c, 2)

            mlp_chunk(0, lambda: transpose_x2(TT - 1))
            with pe.Fori(1, NCH) as c:
                mlp_chunk(c)

        @block.scalar
        def _(act):
            for count in (qk_copied, u_saved, qkT_saved, hid_hi_done):
                act.sem_inc(count, FIRST)

            def copy(out, in_, **kw):
                return act.activation(out, in_, ACT.Copy, **kw)

            def square_x(t, i):
                act.wait_ge(x_in[i], 16 * (t // 2) + 16)
                act.wait_ge(msx_done, t)
                act.wait_ge(ssx_done, t)
                act.activation(junk[:], xin[:, i], ACT.Square, scale=D ** -0.5, accum_out=ssx[:]).then_inc(ssx_done, 1)

            def split_hT(t, i):
                act.wait_ge(xT_done, t + 1)
                copy(hThi[i // 2][:, :, (i % 2) * P:(i % 2) * P + P],
                     psw[:, 0:D].rearrange("p (k c) -> p k c", k=KT)).then_inc(hT_hi, 1)

            def split_wi(k):
                act.wait_ge(w_in_in[k], 16)
                copy(wihi[:, k, 0:QKVW], wraw[:, k, 0:QKVW]).then_inc(wi_hi, 1)

            def split_wi_u(k):
                act.wait_ge(w_u_in[k // (KT // 2)], 16)
                copy(wihi[:, k, QKVW:], wraw[:, k, QKVW:]).then_inc(wi_u_hi, 1)

            def save_qkT(t):
                act.wait_ge(qkT_done, FIRST + t + 1)
                copy(QT[:, :, bass.ds(t * P, P)], psw[:, 3072:3072 + 5 * P].rearrange("p (j c) -> p j c", j=5)
                     ).then_inc(qkT_saved, 1)

            square_x(0, 0)
            split_wi(0)
            square_x(1, 1)
            split_hT(0, 0)
            for k in range(1, 3):
                split_wi(k)
            split_hT(1, 1)
            for k in range(3, 6):
                split_wi(k)
            square_x(2, 0)
            for k in range(6, KT):
                split_wi(k)
            for k in range(KT):
                split_wi_u(k)

            def split_k(seg, kv):
                c0, n = SEQS[seg]
                act.wait_ge(qkT_saved, FIRST + (c0 + n) // P)
                act.wait_ge(ssx_done, TT)
                a = kv * 64
                copy(KA[seg][a:a + 64, kv], QT[a:a + 64, 4, c0:c0 + n]).then_inc(k_hi, 1)

            def split_q(s, pair, idx, unit):
                j = s.job(pair, idx)
                half = s.half_of(idx, unit * s.kts)
                a, c0 = half * 64, s.start + idx // 2 * 512
                if not isinstance(j, int) or j >= 2:
                    act.wait_ge(s_done, GRP * (j - 1))
                if isinstance(j, int) and j == 0 and unit == 0:
                    act.wait_ge(xT_done, TT)
                copy(Qs[a:a + 64, 2 * s.parity(pair, idx) + unit], QT[a:a + 64, bass.ds(pair, 1), c0:c0 + 512]
                     .rearrange("p a c -> p (a c)")).then_inc(q_hi, 1)

            def exps(s, pair, idx, u):
                act.wait_ge(max_done, s.group(pair, idx, u) + 1)
                b = s.parity(pair, idx)
                for h in range(s.tiles):
                    c0, q = h * s.len, u * s.tiles + h
                    ins = act.activation(prob[b][:, u, c0:c0 + s.len],
                                         psw[:, (u % 2) * 1024 + c0:(u % 2) * 1024 + c0 + s.len],
                                         ACT.Exp, bias=nmax[:, b, q:q + 1], accum_out=rsum[:, b, q:q + 1])
                ins.then_inc(exp_done, 1)

            def project_block(n, last):
                for i in range(4):
                    t = n * 4 + i
                    act.wait_ge(qkv_done, t + 1)
                    act.wait_ge(qn_done, FIRST + t)
                    copy(qk[:].rearrange("p h d -> p (h d)"), psw[:, 1024:1024 + QKW]).then_inc(qk_copied, 1)
                    copy(V[:, bass.ds(t, 1), :, 0:HEAD].rearrange("p a v d -> p (a v) d"),
                         ps[:, 3, P:2 * P].rearrange("p (v d) -> p v d", v=NKV)).then_inc(v_hi, 1)
                    act.wait_ge(qk_copied, FIRST + t + 1)
                    act.wait_ge(qk_summed, FIRST + t)
                    act.activation(qksq[:], qk[:], ACT.Square, scale=HEAD ** -0.5).then_inc(qk_squared, 1)
                    if not (last and i >= 2):
                        act.wait_ge(u_done, FIRST + n * 2 + i // 2)
                        split_hT(t + 2, (i + 2) % 4)
                    if not (last and i >= 1):
                        square_x(t + 3, (i + 3) % 2)
                    if last and i == 1:
                        split_k(0, 0)
                        split_k(0, 1)
                        for unit in range(2):
                            split_q(seqs[0], 0, 0, unit)
                    if i % 2:
                        save_qkT(t - 1)
                    if last and i == 3:
                        act.wait_ge(u_done, FIRST + TT // 2 - 1)
                        exps(seqs[0], 0, 0, 0)
                        split_q(seqs[0], 1, 0, 0)
                        exps(seqs[0], 0, 0, 1)
                        split_q(seqs[0], 1, 0, 1)
                        exps(seqs[0], 0, 0, 2)
                    if i % 2:
                        p = n * 2 + i // 2
                        act.wait_ge(u_done, FIRST + p + 1)
                        act.wait_ge(pads, 1)
                        copy(up[:, :, bass.ds(p * 256 + PAD + 2 * PAD * ((n + 1) // 2), 256)],
                             psw[:, 2048:3072].rearrange("p (g c) -> p g c", g=GROUPS)).then_inc(u_saved, 1)
                        save_qkT(t)

            with act.Fori(0, NB - 1) as n:
                project_block(n, False)
            project_block(NB - 1, True)

            def split_p(s, pair, idx, k):
                act.wait_ge(pT_done, s.turn(pair, idx, k) + 1)
                copy(pThi[:, k % 4], ps[:, 4 + k % 3]).then_inc(pT_hi, 1)

            def copy_out(s, pair, idx, half):
                n = s.out(pair, idx, half * (s.n == 0))
                last = s.kts * (half + 1) if s.n == 0 else STEPS
                act.wait_ge(pv_done, s.turn(pair, idx, last))
                if not isinstance(n, int) or n >= 2:
                    act.wait_ge(o_saved, n - 1)
                copy(o_full[:, half], ps[:, 7]).then_inc(o_copied, 1)

            def split_wp():
                act.wait_ge(wp_in, 16)
                act.wait_ge(q_lo[1], 2 * NQ)
                copy(wphi[:], wp_raw[:]).then_inc(wp_hi, 1)

            def split_d(m):
                g, b, c0 = unit_columns(m)
                if m == 0:
                    act.wait_ge(win_step, WINDOW_STEPS)
                if m >= 4:
                    act.wait_ge(z_done, m - 3)
                copy(dhi[:, m % 4], up[:, g, c0:c0 + 512]).then_inc(d_hi, 1)

            def save_z(m):
                g, b, _ = unit_columns(m)
                act.wait_ge(z_done, m + 1)
                copy(concat[:, 4 + g, b * 512:(b + 1) * 512], ps[:, m % 4], scale=pscale[:, g:g + 1]
                     ).then_inc(z_act, 1)

            def split_wo(k):
                act.wait_ge(wo_in[k // 4], 16)
                copy(wohi[:, k], woraw[:, k]).then_inc(wo_hi, 1)

            def attend(s, pair, last=False):
                for idx in range(s.per):
                    for k in range(STEPS):
                        if s.n == 0 and pair < 2 and k == 2:
                            split_k(1, pair)
                        if last and idx == 3:
                            if k:
                                split_d(k + 3)
                            if k % 3 == 0:
                                save_z(k)
                            if k % 3 == 1:
                                split_wo(k // 3)
                        if transposed_in(s, pair, idx, k):
                            split_p(*transposed_in(s, pair, idx, k))
                        if k % s.kts == s.kts - 1:
                            copy_out(s, pair, idx, s.half_of(idx, k))
                        if exped_in(s, pair, idx, k):
                            exps(*exped_in(s, pair, idx, k))
                        if q_split_in(s, pair, idx, k):
                            split_q(*q_split_in(s, pair, idx, k))
                        if last and idx == 2 and k % 2 == 0:
                            split_d(k // 2)
                        if last and idx == 1 and k == 6:
                            split_wp()

            exps(seqs[0], 0, 0, 3)
            split_q(seqs[0], 2, 0, 0)
            act.wait_ge(u_done, FIRST + TT // 2)
            exps(seqs[0], 1, 0, 0)
            split_p(seqs[0], 0, 0, 0)
            split_q(seqs[0], 2, 0, 1)
            split_p(seqs[0], 0, 0, 1)
            exps(seqs[0], 1, 0, 1)
            for pair in range(NQ // 2):
                attend(seqs[0], pair)
            with act.Fori(0, NQ // 2 - 1) as pair:
                attend(seqs[1], pair)
            attend(seqs[1], NQ // 2 - 1, True)

            split_d(11)
            save_z(9)

            def split_c(t, i):
                if not isinstance(t, int) or t >= 2:
                    act.wait_ge(out_done, t - 1)
                copy(chi[:, i], concat[:, :, bass.ds(t * P, P)]).then_inc(c_hi, 1)

            def square_x2(t, i):
                act.wait_ge(x2_done, FIRST + t + 1)
                act.wait_ge(ms2_done, t)
                act.wait_ge(ss2_done, t)
                act.activation(junk2[:], x2in[:, i], ACT.Square, scale=D ** -0.5, accum_out=ssx[:]).then_inc(ss2_done, 1)

            def split_h2(t):
                act.wait_ge(xT2_done, t + 1)
                copy(h2hi[:, :, bass.ds(t * P, P)], psw[:, 2048:3072].rearrange("p (k c) -> p k c", k=KT)
                     ).then_inc(h2_hi, 1)

            def split_wu(c):
                act.wait_ge(wu_in, 16 * c + 16)
                act.wait_ge(up_done, FT * NB * c)
                copy(wuhi[:], wuraw[:]).then_inc(wu_hi, 1)

            act.wait_ge(z_act, GROUPS)
            split_c(0, 0)
            for k in range(3, KT):
                split_wo(k)
            split_c(1, 1)
            act.wait_ge(z_dve, GROUPS * NB - GROUPS)
            act.wait_ge(o_saved, OUTS)
            square_x2(0, 0)
            split_wu(0)
            with act.Fori(0, TT // 2 - 1) as h2:
                t = h2 * 2 + 1
                for i in range(2):
                    split_c(t + i + 1, i % 2)
                    square_x2(t + i, (1 + i) % 2)
                    split_h2(t + i - 1)
            square_x2(TT - 1, 1)
            split_h2(TT - 2)
            split_h2(TT - 1)

            def hidden(c, b):
                for f in range(FT):
                    n = (c * NB + b) * FT + f
                    act.wait_ge(up_done, n + 1)
                    act.wait_ge(sq_done, FIRST + n)
                    act.wait_ge(hid_hi_done, FIRST + n)
                    act.activation(relu[:], ps[:, 6 + f], ACT.Relu).then_inc(relu_done, 1)
                    act.wait_ge(relu_done, n + 1)
                    act.activation(hid_hi[:, b, f], relu[:], ACT.Square).then_inc(hid_hi_done, 1)

            def mlp_chunk(c, last):
                hidden(c, 0)
                act.wait_ge(wd_in, 16 * c + 16)
                act.wait_ge(down_done, FIRST + TT * c)
                copy(wdhi[:], wdraw[:]).then_inc(wd_hi, 1)
                hidden(c, 1)
                hidden(c, 2)
                if not last:
                    split_wu(c + 1)

            act.wait_ge(ss2_done, TT)
            with act.Fori(0, NCH - 1) as c:
                mlp_chunk(c, False)
            mlp_chunk(NCH - 1, True)

        @block.vector
        def _(dve):
            for count in (qk_summed, qn_done, sq_done, v_lo, h2_lo, x2_done, xs2_done, rope_done, cos_done, hid_lo_done):
                dve.sem_inc(count, FIRST)

            def minus(out, a, b):
                return dve.tensor_tensor(out, a, b.bitcast(F32), ALU.subtract)

            def scale_x(t, i):
                dve.wait_ge(rsx_done, t + 1)
                dve.wait_ge(xT_done, t)
                dve.scalar_tensor_tensor(xs[:], xin[:, i], rsx[:, 0:1], g1b[:], ALU.mult, ALU.mult
                                         ).then_inc(xs_done, 1)

            def split_hT(t, i):
                dve.wait_ge(hT_hi, t + 1)
                c0 = (i % 2) * P
                minus(hTlo[i // 2][:, :, c0:c0 + P], psw[:, 0:D].rearrange("p (k c) -> p k c", k=KT),
                      hThi[i // 2][:, :, c0:c0 + P]).then_inc(hT_lo, 1)

            def split_wi(k):
                dve.wait_ge(wi_hi, k + 1)
                minus(wilo[:, k, 0:QKVW], wraw[:, k, 0:QKVW], wihi[:, k, 0:QKVW]).then_inc(wi_lo, 1)

            def split_wi_u(k):
                dve.wait_ge(wi_u_hi, k + 1)
                minus(wilo[:, k, QKVW:], wraw[:, k, QKVW:], wihi[:, k, QKVW:]).then_inc(wi_u_lo, 1)

            dve.wait_ge(g1_in, 16)
            scale_x(0, 0)
            split_wi(0)
            scale_x(1, 1)
            split_hT(0, 0)
            for k in range(1, 3):
                split_wi(k)
            split_hT(1, 1)
            for k in range(3, KT):
                split_wi(k)
            scale_x(2, 0)
            for k in range(KT):
                split_wi_u(k)
            dve.wait_ge(gq_scaled, 1)

            def split_k(seg, kv):
                c0, n = SEQS[seg]
                a = kv * 64
                dve.wait_ge(k_hi, seg * NKV + kv + 1)
                minus(KB[seg][a:a + 64, kv], QT[a:a + 64, 4, c0:c0 + n], KA[seg][a:a + 64, kv]
                      ).then_inc(k_lo, 1)

            def split_q(pair, unit):
                a, b = unit * 64, (1 - unit) * 64
                slot = 2 * (pair % 2) + unit
                dve.wait_ge(q_hi, 2 * pair + unit + 1)
                minus(Qs[b:b + 64, slot], QT[a:a + 64, pair, 0:SEQ_P], Qs[a:a + 64, slot]).then_inc(q_lo[0], 1)

            def maxes(s, pair, idx, u):
                dve.wait_ge(s_done, s.group(pair, idx, u) + 1)
                dve.tensor_reduce(nmax[:, s.parity(pair, idx), u * s.tiles:(u + 1) * s.tiles],
                                  psw[:, (u % 2) * 1024:(u % 2) * 1024 + 1024].rearrange("p (q c) -> p q c", c=s.len),
                                  AX.X, ALU.max, negate=True).then_inc(max_done, 1)

            def inverses(s, pair, idx, u):
                b, q0, q1 = s.parity(pair, idx), u * s.tiles, (u + 1) * s.tiles
                dve.wait_ge(exp_done, s.group(pair, idx, u) + 1)
                dve.reciprocal(rinv[:, b, q0:q1], rsum[:, b, q0:q1]).then_inc(inv_done, 1)

            def project_block(n, last):
                for i in range(4):
                    t = n * 4 + i
                    dve.wait_ge(v_hi, t + 1)
                    minus(V[:, bass.ds(t, 1), :, HEAD:].rearrange("p a v d -> p (a v) d"),
                          ps[:, 3, P:2 * P].rearrange("p (v d) -> p v d", v=NKV),
                          V[:, bass.ds(t, 1), :, 0:HEAD].rearrange("p a v d -> p (a v) d")).then_inc(v_lo, 1)
                    dve.wait_ge(qk_squared, t + 1)
                    dve.wait_ge(msqk_done, FIRST + t)
                    dve.tensor_reduce(ssqk[:], qksq[:], AX.X, ALU.add).then_inc(qk_summed, 1)
                    if not (last and i >= 2):
                        split_hT(t + 2, (i + 2) % 4)
                    if not (last and i >= 1):
                        scale_x(t + 3, (i + 3) % 2)
                    if last and i == 1:
                        split_k(0, 0)
                        split_k(0, 1)
                        split_q(0, 0)
                        split_q(0, 1)
                    if last and i == 3:
                        maxes(seqs[0], 0, 0, 0)
                    dve.wait_ge(rsqk_done, t + 1)
                    dve.wait_ge(sin_done, FIRST + t)
                    dve.tensor_tensor(qn[:], qk[:], rsqk[:].unsqueeze(2).to_broadcast([P, NQK, HEAD]), ALU.mult
                                      ).then_inc(qn_done, 1)
                    dve.wait_ge(qn_done, FIRST + t + 1)
                    dve.tensor_tensor(qn[:], qn[:], gqkb[:], ALU.mult).then_inc(qg_done, 1)
                    if last and i == 3:
                        maxes(seqs[0], 0, 0, 1)
                    dve.wait_ge(qg_done, t + 1)
                    dve.wait_ge(rope_in[i % 2], 16 * (t // 2) + 16)
                    dve.wait_ge(qkT_done, FIRST + t - i % 2)
                    r = roped[:, i % 2]
                    dve.tensor_tensor(r, qn[:], rope[:, i % 2, 0].unsqueeze(1).to_broadcast([P, NQK, HEAD]),
                                      ALU.mult).then_inc(cos_done, 1)
                    dve.wait_ge(cos_done, FIRST + t + 1)
                    dve.wait_ge(sin_done, FIRST + t + 1)
                    dve.tensor_tensor(r, r, qsin[:], ALU.add).then_inc(rope_done, 1)

            with dve.Fori(0, NB - 1) as n:
                project_block(n, False)
            project_block(NB - 1, True)

            def group_values(pair, part):
                k0, k1 = part * 4, part * 4 + 4
                t0 = SEQS[1][0] // P
                dve.tensor_copy(Vg[:, k0:k1], V[:, t0 + k0:t0 + k1, bass.ds(pair_kv(pair), 1), :]
                                .rearrange("p t a d -> p t (a d)").bitcast(F32)).then_inc(vg_done, 1)

            def split_p(s, pair, idx, k):
                dve.wait_ge(pT_hi, s.turn(pair, idx, k) + 1)
                minus(pTlo[:, k % 4], ps[:, 4 + k % 3], pThi[:, k % 4]).then_inc(pT_lo, 1)

            def save_z(m):
                g, b, _ = unit_columns(m)
                dve.wait_ge(z_done, m + 1)
                dve.tensor_scalar(concat[:, 4 + g, b * 512:(b + 1) * 512], ps[:, m % 4],
                                  pscale[:, g:g + 1], None, ALU.mult).then_inc(z_dve, 1)

            def split_wp():
                dve.wait_ge(wp_hi, 1)
                minus(wplo[:], wp_raw[:], wphi[:]).then_inc(wp_lo, 1)

            def split_wo(k):
                dve.wait_ge(wo_hi, k + 1)
                minus(wolo[:, k], woraw[:, k], wohi[:, k]).then_inc(wo_lo, 1)

            def attend(s, pair, last=False):
                for idx in range(s.per):
                    for k in range(STEPS):
                        if s.n == 0 and pair < 2 and k == 4:
                            split_k(1, pair)
                        if s.n == 0 and pair == 2 and k == 2:
                            group_values(0, 0)
                        if last and idx == 2 and k == 4:
                            split_wp()
                        if inverted_in(s, pair, idx, k):
                            inverses(*inverted_in(s, pair, idx, k))
                        if last and idx == 3 and k % 3:
                            save_z(k)
                        if s.n and idx == 0 and k == 1:
                            dve.wait_ge(pv_done, s.turn(pair, 0, 0))
                            group_values(pair, 1)
                        if s.n and idx == 3 and k == 6 and not last:
                            dve.wait_ge(pv_done, s.turn(pair, 3, 4))
                            group_values(pair + 1, 0)
                        if transposed_in(s, pair, idx, k):
                            split_p(*transposed_in(s, pair, idx, k))
                        if scored_in(s, pair, idx, k):
                            maxes(*scored_in(s, pair, idx, k))
                        if k == 6:
                            for kq in (4, 6):
                                q_split = q_split_in(s, pair, idx, kq)
                                if q_split and q_split[0].n == 0:
                                    split_q(q_split[1], q_split[3])

            split_q(1, 0)
            inverses(seqs[0], 0, 0, 0)
            maxes(seqs[0], 0, 0, 2)
            split_q(1, 1)
            inverses(seqs[0], 0, 0, 1)
            maxes(seqs[0], 0, 0, 3)
            inverses(seqs[0], 0, 0, 2)
            maxes(seqs[0], 1, 0, 0)
            inverses(seqs[0], 0, 0, 3)
            split_q(2, 0)
            split_p(seqs[0], 0, 0, 0)
            inverses(seqs[0], 1, 0, 0)
            split_q(2, 1)
            maxes(seqs[0], 1, 0, 1)
            split_p(seqs[0], 0, 0, 1)
            maxes(seqs[0], 1, 0, 2)
            for pair in range(NQ // 2):
                attend(seqs[0], pair)
            with dve.Fori(0, NQ // 2 - 1) as pair:
                attend(seqs[1], pair)
            attend(seqs[1], NQ // 2 - 1, True)

            def split_c(t, i):
                dve.wait_ge(c_hi, t + 1)
                minus(clo[:, i], concat[:, :, bass.ds(t * P, P)], chi[:, i]).then_inc(c_lo, 1)

            def residual(t, i):
                dve.wait_ge(out_done, t + 1)
                dve.wait_ge(x2_in[i], 16 * (t // 2) + 16)
                dve.tensor_tensor(x2in[:, i], x2in[:, i], psw[:, i * 1024:(i + 1) * 1024], ALU.add
                                  ).then_inc(x2_done, 1)

            def scale_x2(t, i):
                dve.wait_ge(rs2_done, t + 1)
                dve.wait_ge(xT2_done, t)
                dve.scalar_tensor_tensor(xs2[:], x2in[:, i], rsx[:, 0:1], g2b[:], ALU.mult, ALU.mult
                                         ).then_inc(xs2_done, 1)

            def split_h2(t):
                dve.wait_ge(h2_hi, t + 1)
                minus(h2lo[:, :, bass.ds(t * P, P)], psw[:, 2048:3072].rearrange("p (k c) -> p k c", k=KT),
                      h2hi[:, :, bass.ds(t * P, P)]).then_inc(h2_lo, 1)

            def split_wu(c):
                dve.wait_ge(wu_hi, c + 1)
                minus(wulo[:], wuraw[:], wuhi[:]).then_inc(wu_lo, 1)

            dve.wait_ge(pv_done, seqs[1].turn(NQ // 2, 0, 0))
            save_z(8)
            split_wo(0)
            split_c(0, 0)
            split_wo(1)
            save_z(10)
            split_wo(2)
            save_z(11)
            for k in range(3, KT):
                split_wo(k)
            split_c(1, 1)
            dve.wait_ge(g2_in, 16)
            residual(0, 0)
            scale_x2(0, 0)
            split_wu(0)
            with dve.Fori(0, TT // 2 - 1) as h2:
                t = h2 * 2 + 1
                for i in range(2):
                    split_c(t + i + 1, i % 2)
                    residual(t + i, (1 + i) % 2)
                    split_h2(t + i - 1)
                    scale_x2(t + i, (1 + i) % 2)
            residual(TT - 1, 1)
            split_h2(TT - 2)
            scale_x2(TT - 1, 1)
            split_h2(TT - 1)

            def hidden(c, b):
                for f in range(FT):
                    n = (c * NB + b) * FT + f
                    dve.wait_ge(relu_done, n + 1)
                    dve.wait_ge(hid_lo_done, FIRST + n)
                    dve.tensor_tensor(hsq[:], relu[:], relu[:], ALU.mult).then_inc(sq_done, 1)
                    dve.wait_ge(sq_done, FIRST + n + 1)
                    dve.wait_ge(hid_hi_done, FIRST + n + 1)
                    minus(hid_lo[:, b, f], hsq[:], hid_hi[:, b, f]).then_inc(hid_lo_done, 1)

            def accumulate(c, b):
                dve.wait_ge(y_in[b], 16)
                for t in range(4 * b, 4 * b + 4):
                    dve.wait_ge(down_done, FIRST + c * TT + t + 1)
                    r = (t % 3) * 1024
                    dve.tensor_tensor(yacc[:, t], yacc[:, t], psw[:, r:r + 1024], ALU.add).then_inc(acc_done, 1)

            def mlp_chunk(c, last):
                hidden(c, 0)
                dve.wait_ge(wd_hi, c + 1)
                minus(wdlo[:], wdraw[:], wdhi[:]).then_inc(wd_lo, 1)
                hidden(c, 1)
                accumulate(c, 0)
                hidden(c, 2)
                accumulate(c, 1)
                if not last:
                    split_wu(c + 1)
                accumulate(c, 2)

            with dve.Fori(0, NCH - 1) as c:
                mlp_chunk(c, False)
            mlp_chunk(NCH - 1, True)

        @block.gpsimd
        def _(pool):
            for count in (msqk_done, sin_done):
                pool.sem_inc(count, FIRST)

            pool.memset(mexp[:], -0.5)
            pool.memset(epsx[:], EPS)
            pool.memset(epsqk[:], EPS).then_inc(mexp_set, 1)
            pool.wait_ge(mexp_set, 1)

            def rsqrt_mean(out, tmp, total, eps, started, done, n):
                pool.tensor_tensor(tmp, total, eps, ALU.add).then_inc(started, 1)
                pool.wait_ge(started, n + 1)
                pool.tensor_tensor(out, tmp, mexp[:, 0:tmp.shape[1]], ALU.pow).then_inc(done, 1)

            def norm_x(t):
                pool.wait_ge(ssx_done, t + 1)
                pool.wait_ge(xs_done, t)
                rsqrt_mean(rsx[:], msx[:], ssx[:], epsx[:], msx_done, rsx_done, t)

            norm_x(0)
            norm_x(1)
            norm_x(2)
            pool.wait_ge(gqk_in, 16)
            pool.tensor_scalar(gqkb[:, 0:NQ], gqkb[:, 0:NQ], SCALE, 1.0, ALU.mult, ALU.mult
                               ).then_inc(gq_scaled, 1)
            pool.memset(up[:], 0.0).then_inc(pads, 1)

            pool.wait_ge(pool_in, 2 * 16)

            steps = [(s, g, m) for s in range(2) for g in range(GROUPS) for m in range(g + 2)]

            def window_step(k):
                s, g, m = steps[k]
                n, w = SEQS[s][1], WINDOWS[g]
                sw = (sw_prompt, sw_sample)[s]
                if k:
                    pool.wait_ge(win_step, k)
                if m <= g:
                    size = n + 2 * PAD - (2 << m) + 1
                    src = up[:, g, UP0[s]:UP0[s] + n + 2 * PAD] if m == 0 else sw[(m + 1) % 2][:]
                    pool.tensor_tensor(sw[m % 2][:, 0:size], src[:, 0:size], src[:, 1 << m:(1 << m) + size],
                                       ALU.add).then_inc(win_step, 1)
                    return
                first = PAD - w // 2
                sums = sw[g % 2][:, first:first + n]
                for e, part in enumerate((sums[:, 0:PAD], sums[:, n - PAD:n])):
                    ins = pool.tensor_tensor(part, part, edge[:, g, e * PAD:(e + 1) * PAD], ALU.mult)
                ins.then_inc(win_edge, 1)
                pool.wait_ge(win_edge, s * GROUPS + g + 1)
                pool.tensor_scalar(sums, sums, 1.0 / w, 1.0, ALU.mult, ALU.mult).then_inc(win_done, 1)
                pool.wait_ge(win_done, s * GROUPS + g + 1)
                c0 = pool_pos(s)
                pool.tensor_tensor(up[:, g, c0:c0 + n], sums, up[:, g, c0:c0 + n], ALU.subtract
                                   ).then_inc(win_step, 1)

            def project_block(n, last):
                for i in range(4):
                    t = n * 4 + i
                    if not (last and i >= 1):
                        norm_x(t + 3)
                    pool.wait_ge(qk_summed, FIRST + t + 1)
                    pool.wait_ge(qn_done, FIRST + t)
                    rsqrt_mean(rsqk[:], msqk[:], ssqk[:], epsqk[:], msqk_done, rsqk_done, FIRST + t)
                    pool.wait_ge(qg_done, t + 1)
                    pool.wait_ge(rope_in[i % 2], 16 * (t // 2) + 16)
                    pool.wait_ge(rope_done, FIRST + t)
                    q4 = qn[:].rearrange("p h (a s f) -> p h a s f", a=2, s=2)
                    o4 = qsin[:].rearrange("p h (a s f) -> p h a s f", a=2, s=2)
                    sn = rope[:, i % 2, 1].rearrange("p (a s f) -> p a s f", a=2, s=2)
                    for to in range(2):
                        ins = pool.tensor_tensor(o4[:, :, :, to], q4[:, :, :, 1 - to],
                                                 sn[:, :, to].unsqueeze(1).to_broadcast([P, NQK, 2, HEAD // 4]),
                                                 ALU.mult)
                    ins.then_inc(sin_done, 1)
                    if last and i:
                        pool.wait_ge(xs_done, TT)
                        pool.wait_ge(u_saved, FIRST + SEQ_P // 256)
                        for k in range(*((0, 5), (5, 11), (11, WINDOW_STEPS // 2))[i - 1]):
                            window_step(k)

            with pool.Fori(0, NB - 1) as n:
                project_block(n, False)
            project_block(NB - 1, True)

            assert len(steps) == WINDOW_STEPS
            done = WINDOW_STEPS // 2

            def normalize(s, pair, idx, u):
                b = s.parity(pair, idx)
                pool.wait_ge(inv_done, s.group(pair, idx, u) + 1)
                for h in range(s.tiles):
                    p = prob[b][:, u, h * s.len:(h + 1) * s.len]
                    q = u * s.tiles + h
                    ins = pool.tensor_scalar(p, p, rinv[:, b, q:q + 1], 1.0, ALU.mult, ALU.mult)
                ins.then_inc(norm_done, 1)

            def split_q(s, pair, idx, normalized):
                a, b = idx % 2 * 64, (1 - idx % 2) * 64
                c0, m = s.start + idx // 2 * 512, s.out(pair, idx, 0) - NQ + 1
                pool.wait_ge(norm_done, normalized)
                if done:
                    pool.wait_ge(win_step, done)
                pool.wait_ge(q_hi, NQ + m)
                pool.tensor_tensor(Qs[b:b + 64, 2 * (idx % 2)], QT[a:a + 64, pair, c0:c0 + 512],
                                   Qs[a:a + 64, 2 * (idx % 2)].bitcast(F32), ALU.subtract).then_inc(q_lo[1], 1)
                pool.wait_ge(q_lo[1], m)

            def add_out(n, normalized):
                half = n % 2
                pair, c0 = (n // 2, 0) if n < NQ else ((n - NQ) // 4, SEQS[1][0] + (n - NQ) % 4 // 2 * 512)
                a = half * 64
                pool.wait_ge(norm_done, normalized)
                if done:
                    pool.wait_ge(win_step, done)
                if n >= OUTS - 2:
                    pool.wait_ge(d_lo, GROUPS * NB)
                pool.wait_ge(o_copied, n + 1)
                pool.wait_ge(o_moved[half], 16 * (n // 2 + 1))
                pool.tensor_tensor(concat[a:a + 64, pair, c0:c0 + 512], o_full[a:a + 64, half],
                                   o_part[a:a + 64], ALU.add).then_inc(o_saved, 1)
                pool.wait_ge(o_saved, n + 1)

            def split_d(m):
                _, _, c0 = unit_columns(m)
                g = m // NB
                pool.wait_ge(d_hi, m + 1)
                pool.tensor_tensor(dlo[:, m % 4], up[:, g, c0:c0 + 512], dhi[:, m % 4].bitcast(F32),
                                   ALU.subtract).then_inc(d_lo, 1)

            for u in range(GRP):
                normalize(seqs[0], 0, 0, u)
            normalize(seqs[0], 1, 0, 0)
            pool.wait_ge(u_saved, FIRST + TT // 2)
            pool.wait_ge(u_done, FIRST + TT // 2)
            for s in seqs:
                for pair in range(NQ // 2):
                    for idx in range(s.per):
                        nxt, nxt2, nxt3 = (later_job(s, pair, idx, a) for a in (1, 2, 3))
                        n, g = s.out(pair, idx, 0), s.group(pair, idx, 0)
                        if nxt:
                            normalize(*nxt, 1)
                            normalize(*nxt, 2)
                        if n and n < OUTS - 1:
                            add_out(n - 1, min(g + GRP + 3, GROUPS_ALL))
                        if nxt:
                            normalize(*nxt, 3)
                        if nxt3 and nxt3[0].n:
                            split_q(*nxt3, g + 2 * GRP)
                        if s.n and done < WINDOW_STEPS:
                            window_step(done)
                            done += 1
                        if nxt2:
                            normalize(*nxt2, 0)
                        elif nxt:
                            for m in range(4):
                                split_d(m)
                        if s.n == 0:
                            add_out(n, g + 2 * GRP + 1)
            for m in range(4, GROUPS * NB):
                split_d(m)
            add_out(OUTS - 2, GROUPS_ALL)
            add_out(OUTS - 1, GROUPS_ALL)

            def norm_x2(t):
                pool.wait_ge(ss2_done, t + 1)
                pool.wait_ge(xs2_done, FIRST + t)
                rsqrt_mean(rsx[:], msx[:], ssx[:], epsx[:], ms2_done, rs2_done, t)

            with pool.Fori(0, TT) as t:
                norm_x2(t)


def rope_tables():
    f32 = np.float32
    n_freq = HEAD // 4
    inv = (f32(THETA) ** (-np.arange(n_freq, dtype=f32) / f32(n_freq))).astype(f32)
    out = []
    for _, n in SEQS:
        pos = np.arange(n)
        ids = np.stack([pos // GRID_W, pos % GRID_W], 1).astype(f32)
        ang = (ids[:, :, None] * inv).astype(f32)
        c, s = np.cos(ang), np.sin(ang)
        out.append(np.stack([np.stack([c, c], 2).reshape(n, HEAD), np.stack([-s, s], 2).reshape(n, HEAD)], 1))
    return np.ascontiguousarray(np.concatenate(out).reshape(TT, P, 2, HEAD).astype(f32))


def edge_table():
    n = 4 * PAD
    out = np.zeros((GROUPS, 2 * PAD), np.float32)
    for g, w in enumerate(WINDOWS):
        t = np.arange(n)
        lo, hi = np.clip(t - w // 2, 0, n), np.clip(t - w // 2 + w, 0, n)
        fix = np.float32(w) / (hi - lo).astype(np.float32)
        out[g] = np.concatenate([fix[:PAD], fix[-PAD:]])
    return np.ascontiguousarray(np.broadcast_to(out, (P, GROUPS, 2 * PAD)))


def kernel(x_prompt, x_sample, norm1_g, w_in, q_norm_g, k_norm_g, w_pool, pool_scale, w_out,
           norm2_g, w_up, w_down):
    import concourse.bacc as bacc
    from concourse.bass_utils import run_bass_kernel_spmd

    a = np.asarray
    gq, gk = a(q_norm_g)[0], a(k_norm_g)[0]
    arrays = {
        "in_x": np.concatenate([a(x_prompt)[0], a(x_sample)[0]]),
        "in_g1": a(norm1_g)[0],
        "in_w_in": a(w_in)[0],
        "in_gqk": np.stack([gq] * NQ + [gk] * NKV),
        "in_w_pool": a(w_pool)[0],
        "in_pool_scale": a(pool_scale)[0].reshape(GROUPS, P).T,
        "in_w_out": a(w_out)[0],
        "in_g2": a(norm2_g)[0],
        "in_w_up": a(w_up)[0].reshape(KT, P, NCH, FC).transpose(2, 1, 0, 3),
        "in_w_down": a(w_down)[0],
        "in_ident": np.eye(P, dtype=np.float32),
        "in_rope": rope_tables(),
        "in_edge": edge_table(),
    }
    arrays = {k: np.ascontiguousarray(v) for k, v in arrays.items()}
    nc = bacc.Bacc("TRN2", target_bir_lowering=False, num_devices=1, dynamic_dma_scratch_size=512)
    args = [nc.dram_tensor(k, v.shape, mybir.dt.from_np(v.dtype), kind="ExternalInput").ap()
            for k, v in arrays.items()]
    y = nc.dram_tensor("out_y", (T, D), F32, kind="ExternalOutput").ap()
    hybrid_layer(nc, *args, y)
    r = run_bass_kernel_spmd(nc, [arrays], core_ids=[0])
    out = r.results[0]["out_y"]
    return out[None, :SEQ_P], out[None, SEQ_P:]
```
